# Optimizing a Trainium2 kernel written in Bass

```python
import jax, jax.numpy as jnp
from jax import lax
import numpy as np

D_MODEL = 1024
BATCH = 1
SEQ = 512
DEPTH = 1

ATT_HEADS = 8
ATT_KV_HEADS = 2
ATT_GROUP = ATT_HEADS // ATT_KV_HEADS
HEAD_DIM = 64
WINDOW = 128
BLOCK = 128
ATT_Q = ATT_HEADS * HEAD_DIM
ATT_KV = ATT_KV_HEADS * HEAD_DIM
RWKV_HEADS = 8
RWKV_HEAD = 64
RWKV_DIM = RWKV_HEADS * RWKV_HEAD
DECAY_LORA = 64
ICLR_LORA = 64
GATE_LORA = 128
N_DIR = 2
GN_EPS = 64e-5
N_BRANCH = 2
N_EXPERTS = 16
EXPERT_FF = 2048
CAPACITY = 2
RMS_EPS = 1e-6

SHIFT_DIM = 3 * RWKV_DIM + N_DIR * DECAY_LORA + N_DIR * ICLR_LORA + GATE_LORA
GATE_DIM = N_BRANCH * D_MODEL
IN_DIM = ATT_Q + 2 * ATT_KV + SHIFT_DIM + GATE_DIM
IN_OFFSETS = (ATT_Q, ATT_Q + ATT_KV, ATT_Q + 2 * ATT_KV, ATT_Q + 2 * ATT_KV + SHIFT_DIM)
RWKV_OFFSETS = (RWKV_DIM, 2 * RWKV_DIM, 3 * RWKV_DIM,
                3 * RWKV_DIM + N_DIR * DECAY_LORA,
                3 * RWKV_DIM + N_DIR * (DECAY_LORA + ICLR_LORA))

kernel_name = "hybrid_swa_rwkv7_ecmoe_adaln"

F32 = jnp.float32

def rmsnorm(x, g):
    xf = x.astype(F32)
    y = xf * lax.rsqrt(jnp.mean(xf * xf, axis=-1, keepdims=True) + RMS_EPS)
    return (y * g.astype(F32)).astype(x.dtype)

def alibi_slopes(n):
    return jnp.exp2(-8.0 * (jnp.arange(n, dtype=F32) + 1.0) / n)

def windowed_attention(q, k, v, sink):
    B, S, _ = q.shape
    nb = S // BLOCK
    qb = q.astype(F32).reshape(B, nb, BLOCK, ATT_KV_HEADS, ATT_GROUP, HEAD_DIM) * (HEAD_DIM ** -0.5)

    def kv_blocks(t):
        t = t.astype(F32).reshape(B, S, ATT_KV_HEADS, HEAD_DIM)
        t = jnp.pad(t, ((0, 0), (BLOCK, BLOCK), (0, 0), (0, 0)))
        t = t.reshape(B, nb + 2, BLOCK, ATT_KV_HEADS, HEAD_DIM)
        return jnp.concatenate([t[:, :-2], t[:, 1:-1], t[:, 2:]], axis=2)

    kb, vb = kv_blocks(k), kv_blocks(v)
    s = jnp.einsum('bnqhgd,bnshd->bnhgqs', qb, kb)
    qi = jnp.arange(BLOCK)[:, None]
    kj = jnp.arange(3 * BLOCK)[None, :]
    dist_i = jnp.abs(qi + BLOCK - kj)
    kpos = jnp.arange(nb)[:, None, None] * BLOCK - BLOCK + kj[None]
    valid = (dist_i[None] <= WINDOW) & (kpos >= 0) & (kpos < S)
    slopes = alibi_slopes(ATT_HEADS).reshape(ATT_KV_HEADS, ATT_GROUP)
    logits = s - slopes[:, :, None, None] * dist_i.astype(F32)
    logits = jnp.where(valid[None, :, None, None], logits, -jnp.inf)
    sk = sink.astype(F32).reshape(1, 1, ATT_KV_HEADS, ATT_GROUP, 1, 1)
    m = jnp.maximum(jnp.max(logits, axis=-1, keepdims=True), sk)
    p = jnp.exp(logits - m)
    p = p / (jnp.sum(p, axis=-1, keepdims=True) + jnp.exp(sk - m))
    o = jnp.einsum('bnhgqs,bnshd->bnqhgd', p, vb)
    return o.reshape(B, S, ATT_Q)

def centred_shift(p, mu):
    prev = jnp.pad(p[:, :-1], ((0, 0), (1, 0), (0, 0)))
    nxt = jnp.pad(p[:, 1:], ((0, 0), (0, 1), (0, 0)))
    return p + mu[0] * (prev - p) + mu[1] * (nxt - p)

def _to_scan(z):
    z = jnp.stack([z[:, :, 0], jnp.flip(z[:, :, 1], axis=1)], axis=2)
    return jnp.transpose(z, (1, 2, 0, 3, 4))

def _wkv7_step(S, inp):
    w, kd, v, nkk, kka, r = inp
    sa = jnp.einsum('dbhvk,dbhk->dbhv', S, nkk)
    S = S * w[..., None, :] + sa[..., None] * kka[..., None, :] + v[..., None] * kd[..., None, :]
    y = jnp.einsum('dbhvk,dbhk->dbhv', S, r)
    return S, y

def rwkv7_bidir(feat, mu, w0, w2, a0, a2, g2, k_k, k_a, r_k, lnx_g, lnx_b):
    B, T, _ = feat.shape
    H, N = RWKV_HEADS, RWKV_HEAD
    f = centred_shift(feat.astype(F32), mu.astype(F32))
    r, k, v, wd, ad, gd = jnp.split(f, RWKV_OFFSETS, axis=-1)
    wd = wd.reshape(B, T, N_DIR, DECAY_LORA)
    ad = ad.reshape(B, T, N_DIR, ICLR_LORA)
    w_log = -jax.nn.softplus(-(w0.astype(F32) + jnp.einsum('btdl,dlc->btdc', jnp.tanh(wd), w2.astype(F32)))) - 0.5
    decay = jnp.exp(-jnp.exp(w_log))
    a = jax.nn.sigmoid(a0.astype(F32) + jnp.einsum('btdl,dlc->btdc', ad, a2.astype(F32)))
    g = jax.nn.sigmoid(gd) @ g2.astype(F32)
    kk = (k * k_k.astype(F32)).reshape(B, T, H, N)
    kk = kk / jnp.maximum(jnp.sqrt(jnp.sum(kk * kk, axis=-1, keepdims=True)), 1e-12)
    kd = (k[:, :, None, :] * (1.0 + (a - 1.0) * k_a.astype(F32))).reshape(B, T, N_DIR, H, N)
    a_h = a.reshape(B, T, N_DIR, H, N)
    rh = r.reshape(B, T, H, N)
    vh = v.reshape(B, T, H, N)
    shp = (B, T, N_DIR, H, N)
    xs = (_to_scan(decay.reshape(shp)),
          _to_scan(kd),
          _to_scan(jnp.broadcast_to(vh[:, :, None], shp)),
          _to_scan(jnp.broadcast_to(-kk[:, :, None], shp)),
          _to_scan(kk[:, :, None] * a_h),
          _to_scan(jnp.broadcast_to(rh[:, :, None], shp)))
    S0 = jnp.zeros((N_DIR, B, H, N, N), F32)
    _, y = lax.scan(_wkv7_step, S0, xs)
    y = jnp.transpose(y, (2, 0, 1, 3, 4))
    y = y[:, :, 0] + jnp.flip(y[:, :, 1], axis=1)
    mean = jnp.mean(y, axis=-1, keepdims=True)
    var = jnp.mean(jnp.square(y - mean), axis=-1, keepdims=True)
    yn = ((y - mean) * lax.rsqrt(var + GN_EPS)).reshape(B, T, RWKV_DIM)
    yn = yn * lnx_g.astype(F32) + lnx_b.astype(F32)
    bonus = jnp.sum(jnp.sum(rh[:, :, None] * kd * r_k.astype(F32), axis=-1, keepdims=True) * vh[:, :, None], axis=2)
    return (yn + bonus.reshape(B, T, RWKV_DIM)) * g

def expert_choice_moe(h, router_w, w_gate, w_up, w_down):
    B, S, D = h.shape
    cap = CAPACITY * S // N_EXPERTS
    aff = jax.nn.softmax(jnp.einsum('bsd,de->bse', h.astype(F32), router_w.astype(F32)), axis=-1)
    gates, idx = lax.top_k(jnp.swapaxes(aff, 1, 2), cap)
    bidx = jnp.arange(B)[:, None, None]
    xe = h[bidx, idx]
    hid = jax.nn.silu(jnp.einsum('becd,edf->becf', xe, w_gate)) * jnp.einsum('becd,edf->becf', xe, w_up)
    ye = jnp.einsum('becf,efd->becd', hid, w_down) * gates[..., None].astype(h.dtype)
    return jnp.zeros_like(h).at[bidx, idx].add(ye.astype(h.dtype))

def setup_inputs(seed: int = 0) -> dict:
    key = jax.random.key(seed)
    ks = jax.random.split(key, 32)
    L, D = DEPTH, D_MODEL
    nrm = lambda k, shp, s: jax.random.normal(k, shp, F32) * s
    return {
        "x": nrm(ks[0], (BATCH, SEQ, D), 1.0),
        "c": nrm(ks[1], (BATCH, D), 1.0),
        "norm1_g": 1.0 + nrm(ks[2], (L, D), 0.05),
        "norm2_g": 1.0 + nrm(ks[3], (L, D), 0.05),
        "ada_w": nrm(ks[4], (L, D, 6 * D), 0.5 * D ** -0.5),
        "ada_b": nrm(ks[5], (L, 6 * D), 0.02),
        "w_in": nrm(ks[6], (L, D, IN_DIM), D ** -0.5),
        "attn_sink": nrm(ks[7], (L, ATT_HEADS), 1.0),
        "shift_mu": jax.random.uniform(ks[8], (L, 2, SHIFT_DIM), F32, 0.0, 0.5),
        "decay_w0": jax.random.uniform(ks[9], (L, N_DIR, RWKV_DIM), F32, -5.0, 0.0),
        "decay_w2": nrm(ks[10], (L, N_DIR, DECAY_LORA, RWKV_DIM), 0.5 * DECAY_LORA ** -0.5),
        "iclr_a0": nrm(ks[11], (L, N_DIR, RWKV_DIM), 0.1),
        "iclr_a2": nrm(ks[12], (L, N_DIR, ICLR_LORA, RWKV_DIM), 0.5 * ICLR_LORA ** -0.5),
        "gate_g2": nrm(ks[13], (L, GATE_LORA, RWKV_DIM), GATE_LORA ** -0.5),
        "k_k": 0.85 + nrm(ks[14], (L, RWKV_DIM), 0.05),
        "k_a": 1.0 + nrm(ks[15], (L, RWKV_DIM), 0.05),
        "r_k": nrm(ks[16], (L, RWKV_HEADS, RWKV_HEAD), 0.1),
        "lnx_g": 1.0 + nrm(ks[17], (L, RWKV_DIM), 0.05),
        "lnx_b": nrm(ks[18], (L, RWKV_DIM), 0.02),
        "w_br_attn": nrm(ks[19], (L, ATT_Q, D), ATT_Q ** -0.5),
        "w_br_rwkv": nrm(ks[20], (L, RWKV_DIM, D), RWKV_DIM ** -0.5),
        "w_out": nrm(ks[21], (L, D, D), D ** -0.5),
        "router_w": nrm(ks[22], (L, D, N_EXPERTS), D ** -0.5),
        "exp_w_gate": nrm(ks[23], (L, N_EXPERTS, D, EXPERT_FF), D ** -0.5),
        "exp_w_up": nrm(ks[24], (L, N_EXPERTS, D, EXPERT_FF), D ** -0.5),
        "exp_w_down": nrm(ks[25], (L, N_EXPERTS, EXPERT_FF, D), EXPERT_FF ** -0.5),
        "final_g": 1.0 + nrm(ks[26], (D,), 0.05),
    }

def reference(x, c, norm1_g, norm2_g, ada_w, ada_b, w_in, attn_sink, shift_mu, decay_w0, decay_w2,
              iclr_a0, iclr_a2, gate_g2, k_k, k_a, r_k, lnx_g, lnx_b, w_br_attn, w_br_rwkv, w_out,
              router_w, exp_w_gate, exp_w_up, exp_w_down, final_g):
    cond = jax.nn.silu(c)
    for l in range(DEPTH):
        mod = (cond @ ada_w[l] + ada_b[l])[:, None, :]
        sh1, sc1, gt1, sh2, sc2, gt2 = jnp.split(mod, 6, axis=-1)
        h = rmsnorm(x, norm1_g[l]) * (1.0 + sc1) + sh1
        proj = h @ w_in[l]
        q, k, v, feat, gl = jnp.split(proj, IN_OFFSETS, axis=-1)
        att = windowed_attention(q, k, v, attn_sink[l]).astype(x.dtype) @ w_br_attn[l]
        rw = rwkv7_bidir(feat, shift_mu[l], decay_w0[l], decay_w2[l], iclr_a0[l], iclr_a2[l],
                         gate_g2[l], k_k[l], k_a[l], r_k[l], lnx_g[l], lnx_b[l]).astype(x.dtype) @ w_br_rwkv[l]
        g_att, g_rw = jnp.split(jax.nn.sigmoid(gl), N_BRANCH, axis=-1)
        mixed = (g_att * att + g_rw * rw) @ w_out[l]
        x = x + (gt1 * mixed).astype(x.dtype)
        h = rmsnorm(x, norm2_g[l]) * (1.0 + sc2) + sh2
        moe = expert_choice_moe(h, router_w[l], exp_w_gate[l], exp_w_up[l], exp_w_down[l])
        x = x + (gt2 * moe).astype(x.dtype)
    return rmsnorm(x, final_g)


_drawn_inputs = setup_inputs


def setup_inputs(seed=0):
    import zlib

    import numpy as np

    out = dict(_drawn_inputs(seed))
    spreads = {}
    factors = {'norm1_g': 5.51,
     'norm2_g': 13.966,
     'ada_b': 4.142,
     'attn_sink': 8.0,
     'decay_w2': 23.492,
     'iclr_a0': 8.0,
     'iclr_a2': 3.48,
     'k_k': 200.0,
     'k_a': 5.877,
     'lnx_g': 200.0,
     'lnx_b': 200.0,
     'decay_w0': 3.429}
    for name, (base, spread) in spreads.items():
        noise = np.random.default_rng([zlib.crc32(name.encode()), seed]).standard_normal(out[name].shape)
        drawn = base * np.exp(spread * noise) if base else spread * noise
        out[name] = __import__('jax').numpy.asarray(drawn.astype(out[name].dtype))
    for name, factor in factors.items():
        out[name] = (out[name] * factor).astype(out[name].dtype)
    return out
```

```python
from contextlib import ExitStack

import concourse.bass as bass
from concourse import mybir

P = 128
D, T = 1024, 512
KC = D // P
TT = T // P
HEADS, KV_HEADS, HD = 8, 2, 64
WINDOW = 128
RH, RN = 8, 64
CH = RH * RN
PAIRS = RH // 2
DIRS = 2
CHUNK = 64
STEPS = T // CHUNK
SUB = 16
LORA = 64
FEAT = 3 * CH + 2 * DIRS * LORA + 128
FB = FEAT // P
QB = HEADS * HD // P
RAWB = QB + 2 + FB
GATEB = 2 * D // P
GATE_COL = RAWB * P
NE, FF = 16, 2048
SLOTS = 2 * T // NE
EPAIRS = NE // 2
FBLK = FF // P
RING = 12
PER_PAIR = 2 * 24
GN_EPS, RMS_EPS = 64e-5, 1e-6
NEG = -1e30
KB = 256

ALU = mybir.AluOpType
ACT = mybir.ActivationFunctionType
AX = mybir.AxisListType
F32 = mybir.dt.float32

MU0, MU1, W0, A0, KKC, KAC, RKC, LG, LB, N1, CC = 0, 15, 30, 38, 46, 50, 54, 58, 62, 66, 74
NPAR = 82


class Signal:

    def __init__(self, sem):
        self.sem, self.n = sem, 0

    def step(self, eng, ins):
        self.n += 1
        ins.then_inc(self.sem, 1)
        eng.wait_ge(self.sem, self.n)


def hybrid_layer(nc, x, c, norm1_g, norm2_g, ada_w, ada_b, w_in, attn_sink, shift_mu, decay_w0,
                 decay_w2, iclr_a0, iclr_a2, gate_g2, k_k, k_a, r_k, lnx_g, lnx_b, w_br_attn,
                 w_br_rwkv, w_out, router_w, exp_w_gate, exp_w_up, exp_w_down, final_g, out):
    ctx = ExitStack()
    with ctx:
        def sb(name, cols, rows=P):
            return ctx.enter_context(nc.sbuf_tensor(name, [rows, cols], F32))[:, :]

        sems = {}

        def sem(name):
            if name not in sems:
                sems[name] = ctx.enter_context(nc.semaphore(name))
            return sems[name]

        mod_rows = nc.dram_tensor("mod_rows", (32, P), F32, kind="Internal").ap()
        rank_rows = nc.dram_tensor("rank_rows", (NE, T), F32, kind="Internal").ap()
        gate_rows = nc.dram_tensor("gate_rows", (NE, T), F32, kind="Internal").ap()

        arena = sb("arena", 194 * KB)

        def at(kb, cols):
            return arena[:, int(kb * KB):int(kb * KB) + cols]

        ident = sb("ident", P)
        head_ones = sb("head_ones", P)
        head_mean = sb("head_mean", P)
        mask_D = sb("mask_D", DIRS * P)
        mask_F = sb("mask_F", DIRS * P)
        mask_DT = sb("mask_DT", DIRS * P)
        mask_AT = sb("mask_AT", DIRS * P)
        mask_QT = sb("mask_QT", DIRS * CHUNK)
        same16 = sb("same16", P)
        half_sel = sb("half_sel", 2)
        neg_dist = sb("neg_dist", 3 * P)
        ones_col = sb("ones_col", P)
        scan_keep = sb("scan_keep", T)
        slot_row = sb("slot_row", SLOTS)
        slot_col = sb("slot_col", 1)
        pcol = sb("pcol", NPAR)
        adab = sb("adab", 48)
        modT = sb("modT", 48)
        cond = sb("cond", KC)
        s1 = sb("s1", KC)
        mu_rest = sb("mu_rest", FB)
        one_minus_ka = sb("one_minus_ka", PAIRS)
        sinks = sb("sinks", HEADS)
        stat = sb("stat", 48)
        att_stat = sb("att_stat", 6 * HEADS)
        Pc = sb("Pc", STEPS * DIRS * PAIRS)
        router_sb = sb("router_sb", KC * NE)

        LW, A_, KD, LC, E_ = (at(o, 16 * KB) for o in (0, 16, 32, 48, 64))
        hT = at(80, 16 * KB)
        attT, GG, BON = at(96, 8 * KB), at(104, 8 * KB), at(112, 8 * KB)
        Vt, Rt, Kt, KKt = at(120, 8 * KB), at(128, 8 * KB), at(136, 8 * KB), at(144, 8 * KB)
        X0 = 152
        x_in = LW
        raw = at(80 - 2 * RAWB, RAWB * T)
        ada_ring = [at(120 + 8 * s, 8 * KB) for s in range(4)]
        ada_acc = at(X0, 24 * KB)
        w_grp = [at(16, 16 * KB), at(96, 16 * KB)]
        par_rows, adab_rows, mod_rows_sb = at(X0 + 24, P), at(X0 + 25, P), at(X0 + 26, P)
        wd_t, ad_t, gd_t = (at(X0 + 24 + 2 * n, T) for n in range(3))
        w2_sb, a2_sb, g2_sb = (at(X0 + 30 + 2 * n, T) for n in range(3))
        kpad = at(X0, 2 * T)
        v_nat = at(X0 + 4, TT * P)
        p_all = at(X0 + 6, HEADS * 3 * P)
        pT = [at(144, 3 * T // 1)[:, 0:3 * P], at(144, 8 * KB)[:, 3 * P:6 * P]]
        o_nat = at(X0 + 18, T)
        names = ["al_bd", "be_bd", "ka_bd", "v_bd", "be_nat", "ka_nat", "v_natp", "AkT", "Qs",
                 "D1", "D1T", "Fm", "Pt", "D2", "D2T"]
        place = {"al_bd": X0, "be_bd": X0 + 4, "ka_bd": X0 + 8, "v_bd": X0 + 12}
        free = [128, 132, 136, 140, 144, 148, X0 + 16, X0 + 20, X0 + 24, X0 + 28, X0 + 32]
        for n, o in zip(names[4:], free):
            place[n] = o
        tile = {n: at(o, 4 * KB) for n, o in place.items()}
        state = at(X0 + 36, 4 * KB)
        rho_s = at(104 + 88, 2 * KB)
        assert X0 + 40 == 192
        yT = at(48, 16 * KB)

        def four(ap):
            return ap.rearrange("p (d m t) -> p d m t", d=DIRS, m=PAIRS)

        def bd(ap):
            return ap.rearrange("p (d m t) -> p d m t", d=DIRS, m=PAIRS)

        def by(ap, n):
            return ap.rearrange("p (n t) -> p n t", n=n)

        w_gate_grp = [at(0, 16 * KB), at(16, 16 * KB)]
        gates = at(128, 32 * KB)
        wba, wbr = at(0, 16 * KB), at(16, 16 * KB)
        wo = at(48, 32 * KB)
        rwT = at(32, 8 * KB)
        gn_tmp = at(40, 8 * KB)
        mixT = at(160, 16 * KB)
        ring = [at(8 * s, 8 * KB) for s in range(RING)]
        x2 = at(96, 16 * KB)
        h2 = at(112, 16 * KB)
        macc = at(128, 16 * KB)
        s2b, sh2b, gt1b, gt2b = (at(144 + 4 * n, D) for n in range(4))
        n2b = at(176, D)
        h2T = at(176, 16 * KB)
        sig = at(144, FF)
        gt2_keep = at(156, D)
        hid = at(160, FF)
        hidT = at(168, FBLK * P)
        xeT = at(176, KC * P)
        ye = at(180, D)
        pick = at(184, TT * 2 * SLOTS)
        rank_b, gate_b, put = at(186, T), at(188, T), at(190, T)
        fin_b = at(152, D)
        affT, work, chosen, count = (at(160 + 2 * n, T)[0:NE, :] for n in range(4))
        aff, affs = at(168, TT * NE), at(169, TT * NE)
        top8 = sb("top8", 8, NE)
        rankT = sb("rankT", TT * NE)

        psum = ctx.enter_context(nc.psum_tensor("psum", [P, 8 * 512], F32))[:, :]

        def bank(b):
            return psum[:, b * 512:(b + 1) * 512]

        def mod_columns(pe, lo, hi):
            pe.wait_ge(sem("ada_used"), KC if hi <= 16 else 3 * KC)
            pe.wait_ge(sem("pcol_ready"), 2)
            for b in range(lo, hi):
                ins = nc.tensor.matmul(psum[:, 256 + b:257 + b], ada_acc[:, b * P:(b + 1) * P],
                                       ones_col[:, 0:1], start=True, stop=True)
            ins.then_inc(sem("mod_mm"), 1)

        def shifted(f):
            if f < 12:
                return by((Rt, Kt, Vt)[f // 4], 4)[:, f % 4, :]
            return (wd_t, ad_t, gd_t)[f - 12]

        copies = ["be_nat", "ka_nat", "v_nat", "D2", "D2T", "D4", "D4T", "D8", "GT", "G", "W", "U1"]
        vecs = ["D1", "F", "DT", "AkT", "Qs", "P1", "P2", "P3", "P4", "H", "QT", "U", "Ssum"]

        def scan_made(eng, i, name, d):
            which, names = ("scan_copies", copies) if name in copies else ("scan_vecs", vecs)
            eng.wait_ge(sem(which), 2 * len(names) * i + 2 * names.index(name) + d + 1)

        def scan_product(eng, i, n, d):
            eng.wait_ge(sem("scan_mm"), 46 * i + 2 * n + d + 1)

        block = ctx.enter_context(nc.Block())

        w_in_v = w_in[0].rearrange("(k p) n -> p k n", p=P)

        @block.sync
        def _(sp):
            load = lambda dst, src, s: sp.dma_start(dst, src).then_inc(sem(s), 16)
            rows = [(MU0, shift_mu[0].rearrange("d (m p) -> (d m) p", p=P)),
                    (W0, decay_w0[0].rearrange("d (m p) -> (d m) p", p=P)),
                    (A0, iclr_a0[0].rearrange("d (m p) -> (d m) p", p=P)),
                    (KKC, k_k.rearrange("l (m p) -> (l m) p", p=P)),
                    (KAC, k_a.rearrange("l (m p) -> (l m) p", p=P)),
                    (RKC, r_k[0].rearrange("(m a) k -> m (a k)", a=2)),
                    (LG, lnx_g.rearrange("l (m p) -> (l m) p", p=P)),
                    (LB, lnx_b.rearrange("l (m p) -> (l m) p", p=P)),
                    (N1, norm1_g.rearrange("l (m p) -> (l m) p", p=P)),
                    (CC, c.rearrange("l (m p) -> (l m) p", p=P))]
            for r, src in rows:
                load(par_rows[r:r + src.shape[0], :], src, "params_in")
            load(adab_rows[0:48, :], ada_b.rearrange("l (m p) -> (l m) p", p=P), "adab_in")
            load(by(x_in, TT), x[0].rearrange("(t p) d -> p t d", p=P), "x_in")

            def ada_piece(n):
                if n >= 4:
                    sp.wait_ge(sem("ada_used"), n - 3)
                load(ada_ring[n % 4], ada_w[0, (n % KC) * P:(n % KC + 1) * P,
                                            (n // KC) * 2048:(n // KC + 1) * 2048], f"ada_in{n % 4}")

            for n in range(KC):
                ada_piece(n)
            for h in range(HEADS):
                col = (h % 4) * P + (h // 4) * HD
                load(by(w_grp[0], KC)[:, :, col:col + HD], w_in_v[:, :, h * HD:(h + 1) * HD], "w_grp0_in")
            load(by(w_grp[1], KC), w_in_v[:, :, 512:1024], "w_grp1_in")
            for n in range(KC, 3 * KC):
                ada_piece(n)
            sp.wait_ge(sem("w2_free"), 1)
            load(w2_sb, decay_w2[0].rearrange("d l c -> (d l) c"), "lora_in")
            load(a2_sb, iclr_a2[0].rearrange("d l c -> (d l) c"), "lora_in")
            load(g2_sb, gate_g2[0], "lora_in")
            load(sinks, attn_sink[0:1, :].partition_broadcast(P), "sinks_in")
            load(by(router_sb, KC), router_w[0].rearrange("(k p) e -> p k e", p=P), "router_in")
            with sp.Fori(0, 2) as it:
                for b in range(2):
                    sp.wait_ge(sem("proj_mm"), 8 * it + 4 * b + 4)
                    load(by(w_grp[b], KC), w_in_v[:, :, bass.ds(1024 * it + 512 * b + 1024, 512)],
                         f"w_grp{b}_in")
            sp.wait_ge(sem("mod_rows_ready"), 1)
            load(mod_rows, mod_rows_sb[0:32, :], "mod_rows_out")
            sp.wait_ge(sem("scan_done"), 1)
            for b in range(2):
                load(by(w_gate_grp[b], KC), w_in_v[:, :, GATE_COL + 512 * b:GATE_COL + 512 * b + 512],
                     f"w_gate{b}_in")
            sp.wait_ge(sem("gn_done"), 1)
            load(by(wo, KC), w_out[0].rearrange("(k p) n -> p k n", p=P), "wo_in")
            for b in range(2):
                sp.wait_ge(sem("gate_mm"), 4 * b + 4)
                load(by(w_gate_grp[b], KC),
                     w_in_v[:, :, GATE_COL + 1024 + 512 * b:GATE_COL + 1536 + 512 * b], f"w_gate{b}_in")
            sp.wait_ge(sem("gate_mm"), GATEB)
            load(by(wba, 4), w_br_attn[0].rearrange("(k p) n -> p k n", p=P), "wbr_in")
            load(by(wbr, 4), w_br_rwkv[0].rearrange("(k p) n -> p k n", p=P), "wbr_in")
            sp.wait_ge(sem("mod_rows_out"), 16)
            sp.wait_ge(sem("mix_mm"), KC)
            row = lambda n: mod_rows[8 * n:8 * n + 8, :].rearrange("(o a) b -> o (a b)", o=1).partition_broadcast(P)
            sp.wait_ge(sem("mixT_ready"), KC)
            load(gt1b, row(0), "rows_in")
            load(sh2b, row(1), "rows_in")
            load(s2b, row(2), "rows_in")
            load(by(x2, TT), x[0].rearrange("(t p) d -> p t d", p=P), "x2_in")
            sp.wait_ge(sem("out_mm"), TT)
            load(n2b, norm2_g[0:1, :].partition_broadcast(P), "n2_in")

            def expert_chunk(i, j):
                kind, k, e = j // 16, (j % 16) // 2, j % 2
                if kind < 2:
                    w = exp_w_up if kind else exp_w_gate
                    src = w[0, bass.ds(2 * i + e, 1), k * P:(k + 1) * P, :].rearrange("o p n -> p (o n)")
                    load(ring[j % RING], src, f"ring{j % RING}_in")
                else:
                    src = exp_w_down[0, bass.ds(2 * i + e, 1), 2 * k * P:(2 * k + 2) * P, :] \
                        .rearrange("o (b p) n -> p (o b) n", p=P)
                    load(by(ring[j % RING], 2), src, f"ring{j % RING}_in")

            for j in range(RING):
                expert_chunk(0, j)
            sp.wait_ge(sem("x2_ready"), TT)
            sp.wait_ge(sem("h2_ready"), TT)
            load(gt2_keep, row(3), "gt2_in")
            load(fin_b, final_g[:].rearrange("(o n) -> o n", o=1).partition_broadcast(P), "fin_in")
            sp.wait_ge(sem("rank_ready"), 1)
            load(rank_rows, count, "route_out")
            load(gate_rows, affT, "route_out")
            sp.wait_ge(sem("route_out"), 32)

            def pair_rows(i):
                for e in range(2):
                    for dst, src in ((rank_b, rank_rows), (gate_b, gate_rows)):
                        load(dst[e * SLOTS:(e + 1) * SLOTS, :],
                             src[bass.ds(2 * i + e, 1), :].partition_broadcast(SLOTS), "pair_rows_in")

            sp.wait_ge(sem("route_lg_done"), 1)
            pair_rows(0)
            with sp.Fori(0, EPAIRS - 1) as i:
                for j in range(RING, PER_PAIR + RING):
                    if j == PER_PAIR:
                        sp.wait_ge(sem("put_ready"), i + 1)
                        sp.sem_inc(sem("rows_free"), 1)
                        pair_rows(i + 1)
                    sp.wait_ge(sem("ring_used"), PER_PAIR * i + (j - RING + 1))
                    sp.sem_inc(sem("ring_reloads"), 1)
                    expert_chunk(i + j // PER_PAIR, j % PER_PAIR)
            last = EPAIRS - 1
            for j in range(RING, PER_PAIR):
                sp.wait_ge(sem("ring_used"), PER_PAIR * last + (j - RING + 1))
                expert_chunk(last, j)
            for t in range(TT):
                sp.wait_ge(sem("final_ready"), t + 1)
                load(out[0, t * P:(t + 1) * P, :], by(h2, TT)[:, t, :], "final_out")
            sp.wait_ge(sem("final_out"), 16 * TT)

        @block.gpsimd
        def _(pool):
            order = Signal(sem("pool_order"))
            s = lambda ins: order.step(pool, ins)

            def select(o, i, pattern, base, cm, fill, op=ALU.is_ge):
                s(nc.gpsimd.affine_select(out=o, in_=i, compare_op=op, fill=fill, base=base,
                                          pattern=pattern, channel_multiplier=cm))

            s(nc.gpsimd.memset(ident, 0.0))
            select(ident, ident, [[-1, P]], 0, 1, 1.0, ALU.not_equal)
            pool.sem_inc(sem("ident_ready"), 1)
            s(nc.gpsimd.memset(ones_col, 1.0))
            for m, v in ((head_ones, 1.0), (head_mean, 1.0 / RN)):
                s(nc.gpsimd.memset(m, 0.0))
                for h in range(2):
                    s(nc.gpsimd.memset(m[h * 64:(h + 1) * 64, h * 64:(h + 1) * 64], v))
            s(nc.gpsimd.memset(half_sel, 0.0))
            for h in range(2):
                s(nc.gpsimd.memset(half_sel[h * 64:(h + 1) * 64, h:h + 1], 1.0))
            s(nc.gpsimd.memset(same16, 1.0))
            v = by(same16, P // SUB)
            select(v, v, [[-SUB, P // SUB], [0, SUB]], 0, 1, 0.0)
            select(v, v, [[SUB, P // SUB], [0, SUB]], SUB - 1, -1, 0.0)
            for m in (mask_F, mask_AT):
                s(nc.gpsimd.memset(m, 0.0))
            s(nc.gpsimd.memset(mask_QT, 1.0))
            for h in range(2):
                r = slice(h * 64, (h + 1) * 64)
                for d in range(2):
                    low = mask_F[r, d * P + h * 64:d * P + (h + 1) * 64]
                    upp = mask_AT[r, d * P + h * 64:d * P + (h + 1) * 64]
                    inc = mask_QT[r, d * 64:(d + 1) * 64]
                    sign = 1 if d == 0 else -1
                    s(nc.gpsimd.memset(low, 1.0))
                    s(nc.gpsimd.memset(upp, 1.0))
                    select(low, low, [[-sign, 64]], -1, sign, 0.0)
                    select(upp, upp, [[sign, 64]], -1, -sign, 0.0)
                    select(inc, inc, [[sign, 64]], 0, -sign, 0.0)
            for d in range(2):
                q = slice(d * P, (d + 1) * P)
                s(nc.gpsimd.tensor_tensor(mask_D[:, q], mask_F[:, q], same16, ALU.mult))
                s(nc.gpsimd.tensor_tensor(mask_DT[:, q], mask_AT[:, q], same16, ALU.mult))
                s(nc.gpsimd.tensor_tensor(mask_F[:, q], mask_F[:, q], mask_D[:, q], ALU.subtract))
            s(nc.gpsimd.memset(scan_keep, 1.0))
            s(nc.gpsimd.memset(by(scan_keep, STEPS)[:, :, 0:1], 0.0))
            s(nc.gpsimd.iota(neg_dist, [[-1, 3 * P]], base=P, channel_multiplier=1,
                             allow_small_or_imprecise_dtypes=True))
            pool.sem_inc(sem("dist_ready"), 1)
            s(nc.gpsimd.iota(slot_row, [[1, SLOTS]], base=0, channel_multiplier=0,
                             allow_small_or_imprecise_dtypes=True))
            for h in range(2):
                s(nc.gpsimd.iota(slot_col[h * 64:(h + 1) * 64, :], [[0, 1]], base=0, channel_multiplier=1,
                                 allow_small_or_imprecise_dtypes=True))
            pool.wait_ge(sem("dist_abs"), 1)
            select(neg_dist, neg_dist, [[1, 3 * P]], 0, -1, NEG)
            select(neg_dist, neg_dist, [[-1, 3 * P]], 2 * P, 1, NEG)
            pool.sem_inc(sem("consts_ready"), 1)

            pool.wait_ge(sem("prep_done"), 1)
            srcs = (("al_bd", four(LW)), ("be_bd", four(A_)), ("ka_bd", four(KD)))
            with pool.Fori(0, STEPS) as i:
                for d in range(DIRS):
                    tok = bass.ds(pool.snap(i * CHUNK if d == 0 else (STEPS - 1) * CHUNK - i * CHUNK), CHUNK)
                    pool.wait_ge(sem("step_used"), 2 * i + d + 1)
                    pool.sem_inc(sem("steps_begun"), 1)
                    for n, src in srcs + (("v_bd", None),):
                        one = (by(Vt, PAIRS)[:, :, tok] if n == "v_bd" else src[:, d, :, tok]).unsqueeze(2)
                        nc.gpsimd.tensor_tensor(
                            bd(tile[n])[:, d].rearrange("p m (h t) -> p m h t", h=2),
                            one.broadcast_to([P, PAIRS, 2, CHUNK]),
                            half_sel.unsqueeze(1).unsqueeze(3).broadcast_to([P, PAIRS, 2, CHUNK]), ALU.mult)
                    nc.gpsimd.tensor_copy(rho_s.rearrange("p (d m t) -> p d m t", d=DIRS, m=PAIRS)[:, d],
                                          four(E_)[:, d, :, tok]).then_inc(sem("operands_ready"), 1)

        @block.tensor
        def _(pe):
            mm = nc.tensor.matmul
            pe.wait_ge(sem("ident_ready"), 1)
            pe.wait_ge(sem("params_in"), 160)
            nc.tensor.transpose(psum[:, 0:NPAR], par_rows[0:NPAR, :], ident[0:NPAR, 0:NPAR]) \
                .then_inc(sem("params_T"), 1)
            pe.wait_ge(sem("adab_in"), 16)
            nc.tensor.transpose(psum[:, 128:176], adab_rows[0:48, :], ident[0:48, 0:48]) \
                .then_inc(sem("params_T"), 1)
            pe.wait_ge(sem("xn_ready"), TT)
            for k in range(KC):
                if k == 7:
                    mod_columns(pe, 0, KC * 2)
                    pe.wait_ge(sem("proj_bank_free"), 1)
                for t in range(TT):
                    ins = nc.tensor.transpose(bank(k % 7 + 1)[:, t * P:(t + 1) * P],
                                              by(x_in, TT)[:, t, k * P:(k + 1) * P], ident)
                ins.then_inc(sem("xT"), 1)

            def project(dst_sem, grp, lhs, idx, mod8, free):
                pe.wait_ge(sem("proj_bank_free"), free)
                for k in range(KC):
                    ins = mm(bank(mod8), lhs(k), by(hT, KC)[:, k, :], start=(k == 0), stop=(k == KC - 1))
                ins.then_inc(sem(dst_sem), 1)

            def plain(g, j):
                return lambda k: by(w_grp[g], KC)[:, k, j * P:(j + 1) * P]

            pe.wait_ge(sem("proj_bank_free"), KC)
            pe.wait_ge(sem("w_grp0_in"), 16 * HEADS)
            for j in range(4):
                project("proj_mm", 0, plain(0, j), j, j, KC)
            with pe.Fori(0, 2) as it:
                for b in range(2):
                    g = 1 - b
                    pe.wait_ge(sem(f"w_grp{g}_in"), 16 * it + (16, 16 * HEADS + 16)[b])
                    for j in range(4):
                        project("proj_mm", g, plain(g, j), None, (4 + 4 * b + j) % 8, 8 * it + 4 + 4 * b + j + 1)
            pe.wait_ge(sem("w_grp1_in"), 48)
            project("proj_mm", 1, plain(1, 0), 20, 4, 21)

            pe.wait_ge(sem("proj_bank_free"), KC + RAWB)
            mod_columns(pe, 16, 48)
            pe.wait_ge(sem("modT_ready"), 2)
            nc.tensor.transpose(bank(1)[0:32, 0:P], modT[:, 16:48], ident).then_inc(sem("modR"), 1)

            pe.wait_ge(sem("lora_in"), 48)
            pe.wait_ge(sem("lora_x"), 3)
            n = 0
            for what in range(2):
                for m in range(PAIRS):
                    for d in range(DIRS):
                        if n >= 6:
                            pe.wait_ge(sem("lora_out"), n - 5)
                        r = slice(d * 64, (d + 1) * 64)
                        mm(bank(2 + n % 6), (w2_sb, a2_sb)[what][r, m * P:(m + 1) * P],
                           (wd_t, ad_t)[what][r, :], start=True, stop=True).then_inc(sem("lora_mm"), 1)
                        n += 1
            for m in range(PAIRS):
                pe.wait_ge(sem("lora_out"), n - 5)
                mm(bank(2 + n % 6), g2_sb[:, m * P:(m + 1) * P], gd_t, start=True, stop=True) \
                    .then_inc(sem("lora_mm"), 1)
                n += 1

            pe.wait_ge(sem("lora_out"), 20)
            pe.wait_ge(sem("mod_rows_ready"), 1)
            for t in range(TT):
                ins = nc.tensor.transpose(bank(7)[:, t * P:(t + 1) * P], by(raw, RAWB)[:, QB + 1, t * P:(t + 1) * P], ident)
            ins.then_inc(sem("vT"), 1)
            pe.wait_ge(sem("kpad_ready"), 3)
            tiles = 0
            for q in range(TT):
                lo, hi = max(q - 1, 0), min(q + 2, TT)
                for h in range(HEADS):
                    n = q * HEADS + h
                    if n >= 4:
                        pe.wait_ge(sem("logits_ready"), n - 3)
                    mm(bank(n % 4)[:, 0:(hi - lo) * P], by(raw, RAWB)[:, h % 4, q * P:(q + 1) * P],
                       by(kpad, 2)[:, h // 4, lo * P:hi * P], start=True, stop=True) \
                        .then_inc(sem("scores_mm"), 1)
                for h in range(HEADS):
                    n = q * HEADS + h
                    pe.wait_ge(sem("probs_ready"), n + 1)
                    if n >= 2:
                        pe.wait_ge(sem("pT_ready"), n - 1)
                    for j in range(hi - lo):
                        ins = nc.tensor.transpose(bank(4 + n % 2)[:, j * P:(j + 1) * P],
                                                  p_all.rearrange("p (h t) -> p h t", h=HEADS)[:, h, j * P:(j + 1) * P], ident)
                    ins.then_inc(sem("pT_mm"), 1)
                    if h == 0 and q:
                        pe.wait_ge(sem("o_ready"), q)
                    pe.wait_ge(sem("pT_ready"), n + 1)
                    for j in range(hi - lo):
                        ins = mm(bank(6)[:, h * HD:(h + 1) * HD], pT[n % 2][:, j * P:(j + 1) * P],
                                 by(v_nat, TT)[:, lo + j, (h // 4) * HD:(h // 4 + 1) * HD],
                                 start=(j == 0), stop=(j == hi - lo - 1))
                    ins.then_inc(sem("pv_mm"), 1)
                pe.wait_ge(sem("o_ready"), q + 1)
                if q:
                    pe.wait_ge(sem("attT_ready"), q)
                for m in range(4):
                    ins = nc.tensor.transpose(bank(7)[:, m * P:(m + 1) * P], o_nat[:, m * P:(m + 1) * P], ident)
                ins.then_inc(sem("attT_mm"), 1)

            pe.wait_ge(sem("attT_ready"), TT)
            pe.wait_ge(sem("kk_sq"), 1)
            for m in range(PAIRS):
                mm(bank(m), head_ones, by(E_[:, 0:8 * KB], PAIRS)[:, m, :], start=True, stop=True) \
                    .then_inc(sem("kk_mm"), 1)
            pe.wait_ge(sem("bonus_in"), 1)
            for m in range(PAIRS):
                mm(bank(4 + m), head_ones, by(E_[:, 8 * KB:16 * KB], PAIRS)[:, m, :], start=True, stop=True) \
                    .then_inc(sem("bonus_mm"), 1)

            B = {n: bd(t) for n, t in tile.items()}
            S_bd = bd(state)
            rho = rho_s.rearrange("p (d m t) -> p d m t", d=DIRS, m=PAIRS)
            Qb = tile["Qs"].rearrange("p (d w m t) -> p w d m t", w=2, d=DIRS, m=PAIRS)
            pe.sem_inc(sem("step_used"), 2)
            with pe.Fori(0, STEPS) as i:
                def product(n, waits, terms, width=P):
                    for d in range(DIRS):
                        for w in waits:
                            if w in ("operands_ready", "y_free", "state_ready"):
                                pe.wait_ge(sem(w), 2 * i + d + 1)
                            else:
                                scan_made(pe, i, w, d)
                        for m in range(PAIRS):
                            o = bank((2 * n + d) % 8)[:, m * width:(m + 1) * width]
                            for a, (lt, rh) in enumerate(terms):
                                ins = mm(o, lt(d, m), rh(d, m), start=(a == 0), stop=(a == len(terms) - 1))
                        ins.then_inc(sem("scan_mm" if n < 23 else "step_used"), 1)

                def t_(n):
                    return lambda d, m: B[n][:, d, m, :]

                idn = lambda d, m: ident
                product(0, ["operands_ready", "state_ready"], [(t_("be_bd"), idn)])
                product(1, [], [(t_("ka_bd"), idn)])
                product(2, ["y_free"], [(t_("v_bd"), idn)])
                product(3, [], [(t_("al_bd"), t_("be_bd"))])
                product(4, ["be_nat"], [(t_("be_bd"), t_("al_bd"))])
                product(5, ["ka_nat"], [(t_("ka_bd"), t_("al_bd"))])
                for d in range(DIRS):
                    scan_made(pe, i, "v_nat", d)
                    for w, src in enumerate(("be_bd", "ka_bd")):
                        for m in range(PAIRS):
                            ins = mm(bank((12 + d) % 8)[:, (w * PAIRS + m) * 64:(w * PAIRS + m + 1) * 64],
                                     B[src][:, d, m, :], rho[:, d, m, :], start=True, stop=True)
                    ins.then_inc(sem("scan_mm"), 1)
                product(7, ["D1", "DT"], [(t_("D1T"), t_("D1"))])
                product(8, ["DT"], [(t_("D1"), t_("D1T"))])
                product(9, ["D2", "P1", "AkT"], [(t_("D2"), t_("Pt"))])
                product(10, ["D2T", "Qs"], [(t_("D2T"), t_("D2"))])
                product(11, [], [(t_("D2"), t_("D2T"))])
                product(12, ["D4", "P2"], [(t_("D1"), t_("Pt"))])
                product(13, ["D4T"], [(t_("D1T"), t_("D1"))])
                product(14, ["D8", "P3"], [(t_("D2"), t_("Pt"))])
                product(15, ["P4"], [(t_("Fm"), t_("Pt"))])
                product(16, [], [(t_("Pt"), t_("Fm"))])
                product(17, ["G", "GT"], [(t_("D1T"), t_("D2T"))])
                product(18, ["H"], [(t_("D1T"), t_("D1"))])
                product(19, [], [(t_("al_bd"), lambda d, m: S_bd[:, d, m, :]),
                                         (t_("AkT"), t_("v_natp"))])
                product(20, ["W"], [(t_("Pt"), t_("Fm"))])
                product(21, ["U1", "QT"], [(t_("D2T"), t_("D1T"))])
                product(22, ["U"],
                        [(lambda d, m: S_bd[:, d, m, :], lambda d, m: rho[:, d, m, :]),
                         (t_("Fm"), lambda d, m: Qb[:, 0, d, m, :]),
                         (t_("v_natp"), lambda d, m: Qb[:, 1, d, m, :])], width=CHUNK)
                product(23, [], [(t_("be_nat"), t_("Fm")), (t_("ka_nat"), t_("v_natp"))])

            pe.wait_ge(sem("y_sum"), 1)
            for m in range(PAIRS):
                mm(bank(m), head_mean, by(yT[:, 0:8 * KB], PAIRS)[:, m, :], start=True, stop=True) \
                    .then_inc(sem("gn_mean_mm"), 1)
            pe.wait_ge(sem("gn_sq"), 1)
            for m in range(PAIRS):
                mm(bank(4 + m), head_mean, by(yT[:, 8 * KB:16 * KB], PAIRS)[:, m, :], start=True, stop=True) \
                    .then_inc(sem("gn_var_mm"), 1)

            for g in range(4):
                pe.wait_ge(sem(f"w_gate{g % 2}_in"), 16 * (g // 2 + 1))
                for j in range(4):
                    idx = 4 * g + j
                    b = idx % 4
                    if idx < 4:
                        pe.wait_ge(sem("gn_centred"), 1)
                    else:
                        pe.wait_ge(sem("gate_ready"), idx - 3)
                    for k in range(KC):
                        ins = mm(bank(b), by(w_gate_grp[g % 2], KC)[:, k, j * P:(j + 1) * P],
                                 by(hT, KC)[:, k, :], start=(k == 0), stop=(k == KC - 1))
                    ins.then_inc(sem("gate_mm"), 1)

            pe.wait_ge(sem("wbr_in"), 32)
            pe.wait_ge(sem("rwT_ready"), 1)
            pe.wait_ge(sem("gate_ready"), GATEB)
            for m in range(KC):
                if m >= 4:
                    pe.wait_ge(sem("mixT_ready"), m - 3)
                for n, (w, src) in enumerate(((wba, attT), (wbr, rwT))):
                    for k in range(4):
                        ins = mm(bank(2 * (m % 4) + n), by(w, 4)[:, k, m * P:(m + 1) * P],
                                 by(src, 4)[:, k, :], start=(k == 0), stop=(k == 3))
                ins.then_inc(sem("mix_mm"), 1)
            pe.wait_ge(sem("wo_in"), 16)
            pe.wait_ge(sem("mixT_ready"), KC)
            for t in range(TT):
                for n in range(2):
                    for k in range(KC):
                        ins = mm(bank(2 * t + n), by(mixT, KC)[:, k, t * P:(t + 1) * P],
                                 by(wo, KC)[:, k, n * 512:(n + 1) * 512], start=(k == 0), stop=(k == KC - 1))
                ins.then_inc(sem("out_mm"), 1)
            pe.wait_ge(sem("h2_ready"), TT)
            for k in range(KC):
                if k >= 4:
                    pe.wait_ge(sem("h2T_ready"), k - 3)
                for t in range(TT):
                    ins = nc.tensor.transpose(bank(k % 4)[:, t * P:(t + 1) * P],
                                              by(h2, TT)[:, t, k * P:(k + 1) * P], ident)
                ins.then_inc(sem("h2T_mm"), 1)
            pe.wait_ge(sem("h2T_ready"), KC)
            pe.wait_ge(sem("router_in"), 16)
            for t in range(TT):
                for k in range(KC):
                    ins = mm(bank(4 + t)[:, 0:NE], by(h2T, KC)[:, k, t * P:(t + 1) * P],
                             by(router_sb, KC)[:, k, :], start=(k == 0), stop=(k == KC - 1))
            ins.then_inc(sem("router_mm"), 1)
            pe.wait_ge(sem("aff_ready"), 1)
            for t in range(TT):
                ins = nc.tensor.transpose(bank(0)[0:NE, t * P:(t + 1) * P], by(aff, TT)[:, t, :], ident)
            ins.then_inc(sem("affT_mm"), 1)
            pe.wait_ge(sem("rank_ready"), 1)
            for t in range(TT):
                ins = nc.tensor.transpose(bank(1)[:, t * NE:(t + 1) * NE], count[:, t * P:(t + 1) * P],
                                          ident[0:NE, 0:NE])
            ins.then_inc(sem("rankT_mm"), 1)

            with pe.Fori(0, EPAIRS) as i:
                pe.wait_ge(sem("pick_ready"), i + 1)
                pe.wait_ge(sem("macc_ready"), 8 * i + 8)
                for k in range(KC):
                    for t in range(TT):
                        ins = mm(bank(k // 4)[:, (k % 4) * P:(k % 4 + 1) * P],
                                 by(h2, TT)[:, t, k * P:(k + 1) * P], by(pick, TT)[:, t, :],
                                 start=(t == 0), stop=(t == TT - 1))
                    if k % 4 == 3:
                        ins.then_inc(sem("xe_mm"), 1)
                pe.wait_ge(sem("xe_ready"), 2 * i + 2)
                for j in range(32):
                    kind, k, e = j // 16, (j % 16) // 2, j % 2
                    pe.wait_ge(sem(f"ring{j % RING}_in"), 64 * i + 16 * (j // RING + 1))
                    for n in range(4):
                        ins = mm(bank(4 * kind + n)[e * 64:(e + 1) * 64, :],
                                 by(xeT, KC)[:, k, e * 64:(e + 1) * 64],
                                 ring[j % RING][:, n * 512:(n + 1) * 512],
                                 start=(k == 0), stop=(k == KC - 1))
                    ins.then_inc(sem("ring_used"), 1)
                for n in range(4):
                    pe.wait_ge(sem("hid_ready"), 4 * i + n + 1)
                    for f in range(4):
                        ins = nc.tensor.transpose(bank(n)[:, f * P:(f + 1) * P],
                                                  hid[:, (4 * n + f) * P:(4 * n + f + 1) * P], ident)
                    ins.then_inc(sem("hidT_mm"), 1)
                for j in range(32, 48):
                    k, e = (j % 16) // 2, j % 2
                    pe.wait_ge(sem(f"ring{j % RING}_in"), 64 * i + 16 * (j // RING + 1))
                    if e == 0 and k % 2 == 0:
                        pe.wait_ge(sem("hidT_ready"), 4 * i + k // 2 + 1)
                    for b in range(2):
                        for n in range(2):
                            ins = mm(bank(4 + n)[e * 64:(e + 1) * 64, :],
                                     by(hidT, FBLK)[:, 2 * k + b, e * 64:(e + 1) * 64],
                                     by(ring[j % RING], 2)[:, b, n * 512:(n + 1) * 512],
                                     start=(k == 0 and b == 0), stop=(k == 7 and b == 1))
                    ins.then_inc(sem("ring_used"), 1)
                pe.wait_ge(sem("ye_ready"), i + 1)
                pe.wait_ge(sem("put_ready"), i + 1)
                for t in range(TT):
                    for n in range(2):
                        mm(bank((6 + 2 * t + n) % 8), put[:, t * P:(t + 1) * P], ye[:, n * 512:(n + 1) * 512],
                           start=True, stop=True).then_inc(sem("put_mm"), 1)

        @block.scalar
        def _(act):
            order = Signal(sem("act_order"))
            fn = nc.scalar.activation
            act.wait_ge(sem("pcol_ready"), 1)
            fn(stat[:, 0:KC], pcol[:, CC:CC + KC], ACT.Sigmoid).then_inc(sem("sig_c"), 1)
            act.wait_ge(sem("x_in"), 16)
            for t in range(TT):
                ins = fn(at(112, D), by(x_in, TT)[:, t, :], ACT.Square, accum_out=stat[:, 8 + t:9 + t])
                order.step(act, ins)
            act.sem_inc(sem("x_sq"), 1)
            act.wait_ge(sem("x_ms"), 1)
            fn(stat[:, 16:20], stat[:, 12:16], ACT.Sqrt).then_inc(sem("x_rms"), 1)
            act.wait_ge(sem("x_rstd"), 1)
            for t in range(TT):
                fn(by(x_in, TT)[:, t, :], by(x_in, TT)[:, t, :], ACT.Copy, scale=stat[:, 20 + t:21 + t]) \
                    .then_inc(sem("xn_ready"), 1)

            rawb = by(raw, RAWB)
            for idx in range(4):
                act.wait_ge(sem("proj_mm"), idx + 1)
                fn(rawb[:, idx, :], bank(idx), ACT.Copy).then_inc(sem("proj_bank_free"), 1)
            with act.Fori(0, 2) as it:
                for j in range(8):
                    act.wait_ge(sem("proj_mm"), 8 * it + 4 + j + 1)
                    fn(raw[:, bass.ds(8 * T * it + (4 + j) * T, T)], bank((4 + j) % 8), ACT.Copy) \
                        .then_inc(sem("proj_bank_free"), 1)
            act.wait_ge(sem("proj_mm"), 21)
            fn(rawb[:, 20, :], bank(4), ACT.Copy).then_inc(sem("proj_bank_free"), 1)
            act.wait_ge(sem("ada_used"), 3 * KC)
            act.wait_ge(sem("mu_ready"), 1)
            act.wait_ge(sem("mod_rows_out"), 16)
            act.wait_ge(sem("proj_bank_free"), KC + RAWB)
            for f in range(FB):
                fn(shifted(f), rawb[:, QB + 2 + f, :], ACT.Copy, scale=mu_rest[:, f:f + 1]) \
                    .then_inc(sem("shift_0"), 1)
            act.wait_ge(sem("shift_done"), FB)
            fn(wd_t, wd_t, ACT.Tanh).then_inc(sem("lora_x"), 1)
            fn(gd_t, gd_t, ACT.Sigmoid).then_inc(sem("lora_x"), 1)
            act.sem_inc(sem("lora_x"), 1)
            n = 0
            for what in range(2):
                for m in range(PAIRS):
                    for d in range(DIRS):
                        act.wait_ge(sem("lora_mm"), n + 1)
                        col = (W0, A0)[what] + 4 * d + m
                        fn(four((LW, A_)[what])[:, d, m, :], bank(2 + n % 6), ACT.Sigmoid,
                           bias=pcol[:, col:col + 1]).then_inc(sem("lora_out"), 1)
                        n += 1
            for m in range(PAIRS):
                act.wait_ge(sem("lora_mm"), n + 1)
                fn(by(GG, PAIRS)[:, m, :], bank(2 + n % 6), ACT.Copy).then_inc(sem("lora_out"), 1)
                n += 1
            pv = p_all.rearrange("p (h t) -> p h t", h=HEADS)
            ast = by(att_stat, 6)
            for q in range(TT):
                nk = min(q + 2, TT) - max(q - 1, 0)
                act.wait_ge(sem("att_max"), q + 1)
                fn(ast[:, 3, :], ast[:, 2, :], ACT.Exp).then_inc(sem("sink_exp"), 1)
                for h in range(HEADS):
                    fn(pv[:, h, 0:nk * P], pv[:, h, 0:nk * P], ACT.Exp, bias=ast[:, 1, h:h + 1],
                       accum_out=ast[:, 4, h:h + 1]).then_inc(sem("probs_ready"), 1)
                act.wait_ge(sem("attT_mm"), q + 1)
                fn(by(attT, 4)[:, :, q * P:(q + 1) * P], by(bank(7), 4), ACT.Copy) \
                    .then_inc(sem("attT_ready"), 1)
            act.wait_ge(sem("kk_raw"), 1)
            fn(E_[:, 0:8 * KB], KKt, ACT.Square).then_inc(sem("kk_sq"), 1)
            for m in range(PAIRS):
                act.wait_ge(sem("kk_mm"), m + 1)
                fn(by(E_[:, 0:8 * KB], PAIRS)[:, m, :], bank(m), ACT.Sqrt).then_inc(sem("kk_norm"), 1)
            act.wait_ge(sem("lc_ready"), 1)
            act.wait_ge(sem("bonus_mm"), 4)
            act.wait_ge(sem("kk_done"), 1)
            fn(E_, LC, ACT.Exp).then_inc(sem("exp_lc"), 1)
            act.wait_ge(sem("lcw_ready"), 1)
            fn(LW, LW, ACT.Exp).then_inc(sem("exp_lcw"), 1)
            act.wait_ge(sem("exp_lc"), 1)
            fn(LC, LC, ACT.Exp, scale=-1.0).then_inc(sem("exp_neg"), 1)

            act.sem_inc(sem("y_free"), 2)
            yv = four(yT)
            B = {n: bd(t) for n, t in tile.items()}

            with act.Fori(0, STEPS) as i:
                def copy_out(n, dst):
                    for d in range(DIRS):
                        scan_product(act, i, n, d)
                        fn(B[dst][:, d], by(bank((2 * n + d) % 8), PAIRS), ACT.Copy).then_inc(sem("scan_copies"), 1)

                copy_out(0, "be_nat")
                copy_out(1, "ka_nat")
                copy_out(2, "v_natp")
                copy_out(7, "D2")
                copy_out(8, "D2T")
                copy_out(10, "D1")
                copy_out(11, "D1T")
                copy_out(13, "D2")
                copy_out(15, "D2T")
                copy_out(16, "D1T")
                copy_out(19, "Fm")
                copy_out(20, "D1T")
                for d in range(DIRS):
                    tok = bass.ds(i * CHUNK if d == 0 else (STEPS - 1) * CHUNK - i * CHUNK, CHUNK)
                    scan_product(act, i, 22, d)
                    fn(yv[:, d, :, tok], bank((44 + d) % 8)[:, 0:PAIRS * CHUNK].rearrange("p (m t) -> p m t", m=PAIRS),
                       ACT.Copy).then_inc(sem("y_free"), 1)

            act.wait_ge(sem("gn_centred"), 1)
            fn(yT[:, 8 * KB:16 * KB], yT[:, 0:8 * KB], ACT.Square).then_inc(sem("gn_sq"), 1)
            act.wait_ge(sem("gn_vare"), 4)
            fn(gn_tmp, gn_tmp, ACT.Sqrt).then_inc(sem("gn_std"), 1)
            for idx in range(GATEB):
                act.wait_ge(sem("gate_mm"), idx + 1)
                fn(by(gates, GATEB)[:, idx, :], bank(idx % 4), ACT.Sigmoid).then_inc(sem("gate_ready"), 1)
            for t in range(TT):
                act.wait_ge(sem("x2_ready"), t + 1)
                fn(at(180, D), by(x2, TT)[:, t, :], ACT.Square, accum_out=stat[:, 8 + t:9 + t]) \
                    .then_inc(sem("x2_sq"), 1)
                act.wait_ge(sem("x2_sq"), t + 1)
            act.wait_ge(sem("x2_ms"), 1)
            fn(stat[:, 16:20], stat[:, 12:16], ACT.Sqrt).then_inc(sem("x2_rms"), 1)
            act.wait_ge(sem("h2_ready"), TT)
            for k in range(KC):
                act.wait_ge(sem("h2T_mm"), k + 1)
                fn(by(h2T, KC)[:, k, :], bank(k % 4), ACT.Copy).then_inc(sem("h2T_ready"), 1)
            act.wait_ge(sem("lg_ready"), 1)
            fn(affs, affs, ACT.Exp).then_inc(sem("aff_exp"), 1)
            act.wait_ge(sem("affT_mm"), 1)
            fn(affT, bank(0)[0:NE, :], ACT.Copy).then_inc(sem("affT_ready"), 1)
            with act.Fori(0, EPAIRS) as i:
                for g in range(2):
                    act.wait_ge(sem("xe_mm"), 2 * i + g + 1)
                    fn(xeT[:, g * 512:(g + 1) * 512], bank(g), ACT.Copy).then_inc(sem("xe_ready"), 1)
                act.wait_ge(sem("ring_used"), PER_PAIR * i + 16)
                for n in range(4):
                    fn(sig[:, n * 512:(n + 1) * 512], bank(n), ACT.Sigmoid).then_inc(sem("sig_ready"), 1)
                for n in range(4):
                    act.wait_ge(sem("hidT_mm"), 4 * i + n + 1)
                    fn(hidT[:, n * 512:(n + 1) * 512], bank(n), ACT.Copy).then_inc(sem("hidT_ready"), 1)
                act.wait_ge(sem("ring_used"), PER_PAIR * i + PER_PAIR)
                fn(ye, psum[:, 4 * 512:6 * 512], ACT.Copy).then_inc(sem("ye_ready"), 1)
            for t in range(TT):
                act.wait_ge(sem("x3_ready"), t + 1)
                fn(at(160, D), by(x2, TT)[:, t, :], ACT.Square, accum_out=stat[:, 24 + t:25 + t]) \
                    .then_inc(sem("x3_sq"), 1)
                act.wait_ge(sem("x3_sq"), t + 1)
            act.wait_ge(sem("x3_ms"), 1)
            fn(stat[:, 32:36], stat[:, 28:32], ACT.Sqrt).then_inc(sem("x3_rms"), 1)

        @block.vector
        def _(dve):
            v = nc.vector
            order = Signal(sem("dve_order"))
            s = lambda ins: order.step(dve, ins)
            dve.wait_ge(sem("params_T"), 2)
            v.tensor_copy(pcol, psum[:, 0:NPAR]).then_inc(sem("pcol_ready"), 1)
            v.tensor_copy(adab, psum[:, 128:176]).then_inc(sem("pcol_ready"), 1)
            dve.wait_ge(sem("pcol_ready"), 2)
            s(v.tensor_tensor(mu_rest, pcol[:, MU0:MU0 + FB], pcol[:, MU1:MU1 + FB], ALU.add))
            v.tensor_scalar(mu_rest, mu_rest, -1.0, 1.0, ALU.mult, ALU.add).then_inc(sem("mu_ready"), 1)
            s(v.tensor_scalar(one_minus_ka, pcol[:, KAC:KAC + 4], -1.0, 1.0, ALU.mult, ALU.add))
            dve.wait_ge(sem("sig_c"), 1)
            s(v.tensor_tensor(cond, pcol[:, CC:CC + KC], stat[:, 0:KC], ALU.mult))
            dve.wait_ge(sem("dist_ready"), 1)
            dist_tmp = at(116, 3 * P)
            s(v.tensor_scalar(dist_tmp, neg_dist, -1.0, None, ALU.mult))
            v.tensor_tensor(dist_tmp, dist_tmp, neg_dist, ALU.min).then_inc(sem("dist_min"), 1)

            def ada(n):
                dve.wait_ge(sem(f"ada_in{n % 4}"), 16 * (n // 4 + 1))
                k, part = n % KC, ada_acc[:, (n // KC) * 2048:(n // KC + 1) * 2048]
                if k == 0:
                    ins = v.tensor_scalar(part, ada_ring[n % 4], cond[:, 0:1], None, ALU.mult)
                else:
                    dve.wait_ge(sem("ada_used"), n)
                    ins = v.scalar_tensor_tensor(part, ada_ring[n % 4], cond[:, k:k + 1], part, ALU.mult, ALU.add)
                ins.then_inc(sem("ada_used"), 1)

            def rstd(src, ms_sem, rms_sem, base):
                v.tensor_scalar(stat[:, base + 4:base + 8], stat[:, base:base + 4], 1.0 / D, RMS_EPS,
                                ALU.mult, ALU.add).then_inc(sem(ms_sem), 1)
                dve.wait_ge(sem(rms_sem), 1)
                return v.reciprocal(stat[:, base + 12:base + 16], stat[:, base + 8:base + 12])

            dve.wait_ge(sem("dist_min"), 1)
            v.tensor_copy(neg_dist, dist_tmp).then_inc(sem("dist_abs"), 1)
            dve.wait_ge(sem("x_sq"), 1)
            rstd(None, "x_ms", "x_rms", 8).then_inc(sem("x_rstd"), 1)
            for n in range(KC):
                ada(n)
            dve.wait_ge(sem("mod_mm"), 1)
            v.tensor_tensor(modT[:, 0:16], psum[:, 256:272], adab[:, 0:16], ALU.add).then_inc(sem("modT_ready"), 1)
            dve.wait_ge(sem("modT_ready"), 1)
            s(v.tensor_scalar(s1, modT[:, KC:2 * KC], 1.0, None, ALU.add))
            s(v.tensor_tensor(s1, s1, pcol[:, N1:N1 + KC], ALU.mult))
            for k in range(KC):
                dve.wait_ge(sem("xT"), k + 1)
                v.tensor_scalar(by(hT, KC)[:, k, :], bank(k % 7 + 1), s1[:, k:k + 1], modT[:, k:k + 1],
                                ALU.mult, ALU.add).then_inc(sem("proj_bank_free"), 1)
            for n in range(KC, 3 * KC):
                ada(n)
            dve.sem_inc(sem("w2_free"), 1)
            dve.wait_ge(sem("mod_mm"), 2)
            v.tensor_tensor(modT[:, 16:48], psum[:, 272:304], adab[:, 16:48], ALU.add) \
                .then_inc(sem("modT_ready"), 1)
            dve.wait_ge(sem("modR"), 1)
            v.tensor_copy(mod_rows_sb[0:32, :], bank(1)[0:32, 0:P]).then_inc(sem("mod_rows_ready"), 1)

            rawb = by(raw, RAWB)
            for f in [12, 13, 14] + list(range(12)):
                dve.wait_ge(sem("shift_0"), FB)
                p = rawb[:, QB + 2 + f, :]
                o = shifted(f)
                s(v.scalar_tensor_tensor(o[:, 1:T], p[:, 0:T - 1], pcol[:, MU0 + f:MU0 + f + 1], o[:, 1:T],
                                         ALU.mult, ALU.add))
                v.scalar_tensor_tensor(o[:, 0:T - 1], p[:, 1:T], pcol[:, MU1 + f:MU1 + f + 1], o[:, 0:T - 1],
                                       ALU.mult, ALU.add).then_inc(sem("shift_done"), 1)

            dve.wait_ge(sem("mod_mm"), 2)
            q_all = raw[:, 0:QB * T]
            v.tensor_scalar(q_all, q_all, HD ** -0.5, None, ALU.mult).then_inc(sem("kpad_ready"), 1)
            dve.wait_ge(sem("consts_ready"), 1)
            for h in range(2):
                ins = v.tensor_scalar(by(kpad, 2)[:, h, :], rawb[:, QB, :], half_sel[:, h:h + 1], None, ALU.mult)
            ins.then_inc(sem("kpad_ready"), 1)
            dve.wait_ge(sem("vT"), 1)
            v.tensor_copy(v_nat, bank(7)).then_inc(sem("kpad_ready"), 1)
            dve.wait_ge(sem("sinks_in"), 16)
            pv = p_all.rearrange("p (h t) -> p h t", h=HEADS)
            ast = by(att_stat, 6)
            for q in range(TT):
                lo, hi = max(q - 1, 0), min(q + 2, TT)
                w = (hi - lo) * P
                band = slice((lo - q + 1) * P, (hi - q + 1) * P)
                if q:
                    dve.wait_ge(sem("pT_mm"), HEADS * q)
                for h in range(HEADS):
                    dve.wait_ge(sem("scores_mm"), q * HEADS + h + 1)
                    v.scalar_tensor_tensor(pv[:, h, 0:w], neg_dist[:, band], 2.0 ** -(h + 1),
                                           bank((q * HEADS + h) % 4)[:, 0:w], ALU.mult, ALU.add) \
                        .then_inc(sem("logits_ready"), 1)
                dve.wait_ge(sem("logits_ready"), HEADS * (q + 1))
                s(v.tensor_reduce(ast[:, 0, :], pv[:, :, 0:w], AX.X, ALU.max))
                s(v.tensor_tensor(ast[:, 0, :], ast[:, 0, :], sinks, ALU.max))
                s(v.tensor_tensor(ast[:, 2, :], sinks, ast[:, 0, :], ALU.subtract))
                v.tensor_scalar(ast[:, 1, :], ast[:, 0, :], -1.0, None, ALU.mult).then_inc(sem("att_max"), 1)
                for h in range(HEADS):
                    n = q * HEADS + h
                    dve.wait_ge(sem("pT_mm"), n + 1)
                    if n >= 2:
                        dve.wait_ge(sem("pv_mm"), n - 1)
                    v.tensor_copy(pT[n % 2][:, 0:w], bank(4 + n % 2)[:, 0:w]).then_inc(sem("pT_ready"), 1)
                dve.wait_ge(sem("sink_exp"), q + 1)
                dve.wait_ge(sem("probs_ready"), HEADS * (q + 1))
                s(v.tensor_tensor(ast[:, 5, :], ast[:, 4, :], ast[:, 3, :], ALU.add))
                s(v.reciprocal(ast[:, 5, :], ast[:, 5, :]))
                dve.wait_ge(sem("pv_mm"), HEADS * (q + 1))
                if q:
                    dve.wait_ge(sem("attT_mm"), q)
                v.tensor_tensor(by(o_nat, HEADS), by(bank(6), HEADS),
                                ast[:, 5, :].unsqueeze(2).broadcast_to([P, HEADS, HD]), ALU.mult) \
                    .then_inc(sem("o_ready"), 1)
            dve.wait_ge(sem("attT_mm"), TT)

            for m in range(PAIRS):
                s(v.tensor_scalar(by(KKt, 4)[:, m, :], by(Kt, 4)[:, m, :], pcol[:, KKC + m:KKC + m + 1], None, ALU.mult))
            dve.sem_inc(sem("kk_raw"), 1)
            dve.wait_ge(sem("lora_out"), 20)
            s(v.tensor_scalar(LW, LW, -float(2.718281828459045 ** -0.5), None, ALU.mult))
            for d in range(DIRS):
                for m in range(PAIRS):
                    s(v.tensor_scalar(four(KD)[:, d, m, :], four(A_)[:, d, m, :], pcol[:, KAC + m:KAC + m + 1],
                                      one_minus_ka[:, m:m + 1], ALU.mult, ALU.add))
                s(v.tensor_tensor(KD[:, d * 2048:(d + 1) * 2048], KD[:, d * 2048:(d + 1) * 2048], Kt, ALU.mult))
            bon = E_[:, 8 * KB:16 * KB]
            s(v.tensor_tensor(bon, KD[:, 0:2048], KD[:, 2048:4096], ALU.add))
            for m in range(PAIRS):
                s(v.scalar_tensor_tensor(by(bon, 4)[:, m, :], by(Rt, 4)[:, m, :], pcol[:, RKC + m:RKC + m + 1],
                                         by(bon, 4)[:, m, :], ALU.mult, ALU.mult))
            dve.sem_inc(sem("bonus_in"), 1)
            dve.wait_ge(sem("kk_norm"), 4)
            nrm = E_[:, 0:8 * KB]
            s(v.tensor_scalar(nrm, nrm, 1e-12, None, ALU.max))
            s(v.reciprocal(nrm, nrm))
            s(v.tensor_tensor(KKt, KKt, nrm, ALU.mult))
            for m in range(PAIRS):
                dve.wait_ge(sem("bonus_mm"), m + 1)
                s(v.tensor_tensor(by(BON, 4)[:, m, :], bank(4 + m), by(Vt, 4)[:, m, :], ALU.mult))
            dve.sem_inc(sem("kk_done"), 1)
            for d in range(DIRS):
                for m in range(PAIRS):
                    s(v.tensor_tensor_scan(four(LC)[:, d, m, :], scan_keep, four(LW)[:, d, m, :], 0.0,
                                           ALU.mult, ALU.add))
            back = LC[:, 2048:4096].rearrange("p (c t) -> p c t", t=CHUNK)
            tot = at(104 + 88, 32).unsqueeze(2)
            s(v.tensor_copy(tot, back[:, :, CHUNK - 1:CHUNK]))
            s(v.tensor_tensor(back, tot.broadcast_to([P, 32, CHUNK]), back, ALU.subtract))
            s(v.tensor_tensor(LC[:, 2048:4096], LC[:, 2048:4096], LW[:, 2048:4096], ALU.add))
            dve.sem_inc(sem("lc_ready"), 1)
            s(v.tensor_tensor(LW, LC, LW, ALU.subtract))
            dve.sem_inc(sem("lcw_ready"), 1)
            for d in range(DIRS):
                h = slice(d * 2048, (d + 1) * 2048)
                s(v.tensor_tensor(A_[:, h], A_[:, h], KKt, ALU.mult))
            dve.wait_ge(sem("exp_lc"), 1)
            pcv = Pc.rearrange("p (s d m) -> p d m s", s=STEPS, d=DIRS)
            e5 = E_.rearrange("p (d m s t) -> p d m s t", d=DIRS, m=PAIRS, s=STEPS)
            s(v.tensor_copy(pcv[:, 0], e5[:, 0, :, :, CHUNK - 1]))
            for st in range(STEPS):
                s(v.tensor_copy(pcv[:, 1, :, st], e5[:, 1, :, STEPS - 1 - st, 0]))
            for d in range(DIRS):
                h = slice(d * 2048, (d + 1) * 2048)
                s(v.tensor_tensor(E_[:, h], E_[:, h], Rt, ALU.mult))
            dve.wait_ge(sem("exp_lcw"), 1)
            for d in range(DIRS):
                h = slice(d * 2048, (d + 1) * 2048)
                s(v.scalar_tensor_tensor(LW[:, h], LW[:, h], -1.0, KKt, ALU.mult, ALU.mult))
            dve.wait_ge(sem("exp_neg"), 1)
            s(v.tensor_tensor(A_, A_, LC, ALU.mult))
            s(v.tensor_tensor(KD, KD, LC, ALU.mult))
            dve.sem_inc(sem("prep_done"), 1)

            B = {n: bd(t) for n, t in tile.items()}
            S_bd = bd(state)
            s(v.memset(state, 0.0))
            dve.sem_inc(sem("state_ready"), 2)
            Qb = tile["Qs"].rearrange("p (d x t) -> p d x t", d=DIRS, t=CHUNK)
            with dve.Fori(0, STEPS) as i:
                def masked(n, d, dst, mask):
                    scan_product(dve, i, n, d)
                    v.tensor_tensor(B[dst][:, d], by(bank((2 * n + d) % 8), PAIRS),
                                    mask[:, d * P:(d + 1) * P].unsqueeze(1).broadcast_to([P, PAIRS, P]),
                                    ALU.mult).then_inc(sem("scan_vecs"), 1)

                def plus(n, dst, add):
                    for d in range(DIRS):
                        scan_product(dve, i, n, d)
                        v.tensor_tensor(B[dst][:, d], by(bank((2 * n + d) % 8), PAIRS), B[add][:, d], ALU.add) \
                            .then_inc(sem("scan_vecs"), 1)

                for d in range(DIRS):
                    masked(3, d, "D1", mask_D)
                for d in range(DIRS):
                    masked(3, d, "Fm", mask_F)
                for d in range(DIRS):
                    masked(4, d, "D1T", mask_DT)
                for d in range(DIRS):
                    masked(5, d, "AkT", mask_AT)
                for d in range(DIRS):
                    scan_product(dve, i, 6, d)
                    v.tensor_tensor(Qb[:, d], by(bank((12 + d) % 8), 8),
                                    mask_QT[:, d * 64:(d + 1) * 64].unsqueeze(1).broadcast_to([P, 8, 64]),
                                    ALU.mult).then_inc(sem("scan_vecs"), 1)
                for d in range(DIRS):
                    scan_made(dve, i, "DT", d)
                    v.tensor_tensor(B["Pt"][:, d], B["D1T"][:, d],
                                    ident.unsqueeze(1).broadcast_to([P, PAIRS, P]), ALU.add) \
                        .then_inc(sem("scan_vecs"), 1)
                plus(9, "Pt", "Pt")
                plus(12, "Pt", "Pt")
                plus(14, "Pt", "Pt")
                for d in range(DIRS):
                    scan_made(dve, i, "GT", d)
                plus(17, "D1", "D2T")
                plus(18, "D2T", "D2T")
                for d in range(DIRS):
                    scan_made(dve, i, "U1", d)
                    scan_product(dve, i, 21, d)
                    v.tensor_tensor(B["Fm"][:, d], by(bank((42 + d) % 8), PAIRS), B["D1T"][:, d], ALU.add) \
                        .then_inc(sem("scan_vecs"), 1)
                for d in range(DIRS):
                    dve.wait_ge(sem("step_used"), 2 * i + d + 3)
                    v.tensor_tensor(S_bd[:, d], by(bank((46 + d) % 8), PAIRS), S_bd[:, d], ALU.add) \
                        .then_inc(sem("scan_vecs"), 1)
                for d in range(DIRS):
                    scan_made(dve, i, "Ssum", d)
                    pc = Pc[:, bass.ds(i * DIRS * PAIRS + d * PAIRS, PAIRS)]
                    v.tensor_tensor(S_bd[:, d], S_bd[:, d], pc.unsqueeze(2).broadcast_to([P, PAIRS, P]),
                                    ALU.mult).then_inc(sem("state_ready"), 1)

            dve.wait_ge(sem("y_free"), 2 * STEPS + 2)
            dve.wait_ge(sem("step_used"), 2 * STEPS + 2)
            dve.sem_inc(sem("scan_done"), 1)
            y = yT[:, 0:8 * KB]
            s(v.tensor_tensor(y, y, yT[:, 8 * KB:16 * KB], ALU.add))
            dve.sem_inc(sem("y_sum"), 1)
            for m in range(PAIRS):
                dve.wait_ge(sem("gn_mean_mm"), m + 1)
                s(v.scalar_tensor_tensor(by(y, 4)[:, m, :], bank(m), -1.0, by(y, 4)[:, m, :], ALU.mult, ALU.add))
            dve.sem_inc(sem("gn_centred"), 1)
            for m in range(PAIRS):
                dve.wait_ge(sem("gn_var_mm"), m + 1)
                v.tensor_scalar(by(gn_tmp, 4)[:, m, :], bank(4 + m), GN_EPS, None, ALU.add) \
                    .then_inc(sem("gn_vare"), 1)
            dve.wait_ge(sem("gn_std"), 1)
            s(v.reciprocal(gn_tmp, gn_tmp))
            s(v.tensor_tensor(rwT, y, gn_tmp, ALU.mult))
            dve.sem_inc(sem("gn_done"), 1)
            for m in range(PAIRS):
                s(v.tensor_scalar(by(rwT, 4)[:, m, :], by(rwT, 4)[:, m, :], pcol[:, LG + m:LG + m + 1],
                                  pcol[:, LB + m:LB + m + 1], ALU.mult, ALU.add))
            s(v.tensor_tensor(rwT, rwT, BON, ALU.add))
            v.tensor_tensor(rwT, rwT, GG, ALU.mult).then_inc(sem("rwT_ready"), 1)
            tmp = [at(40, T), at(42, T)]
            gv = by(gates, GATEB)
            for m in range(KC):
                dve.wait_ge(sem("mix_mm"), m + 1)
                if m:
                    dve.wait_ge(sem("mixT_ready"), m)
                s(v.tensor_tensor(tmp[0], gv[:, m, :], bank(2 * (m % 4)), ALU.mult))
                s(v.tensor_tensor(tmp[1], gv[:, KC + m, :], bank(2 * (m % 4) + 1), ALU.mult))
                v.tensor_tensor(by(mixT, KC)[:, m, :], tmp[0], tmp[1], ALU.add).then_inc(sem("mixT_ready"), 1)
            dve.wait_ge(sem("rows_in"), 48)
            dve.wait_ge(sem("x2_in"), 16)
            t1 = at(128, D)
            for t in range(TT):
                dve.wait_ge(sem("out_mm"), t + 1)
                if t:
                    dve.wait_ge(sem("x2_ready"), t)
                s(v.tensor_tensor(t1, psum[:, 1024 * t:1024 * t + 1024], gt1b, ALU.mult))
                v.tensor_tensor(by(x2, TT)[:, t, :], by(x2, TT)[:, t, :], t1, ALU.add) \
                    .then_inc(sem("x2_ready"), 1)
            dve.wait_ge(sem("n2_in"), 16)
            s(v.scalar_tensor_tensor(s2b, s2b, 1.0, n2b, ALU.add, ALU.mult))
            dve.wait_ge(sem("x2_sq"), TT)
            s(rstd(None, "x2_ms", "x2_rms", 8))
            for t in range(TT):
                s(v.scalar_tensor_tensor(by(h2, TT)[:, t, :], by(x2, TT)[:, t, :], stat[:, 20 + t:21 + t], s2b,
                                         ALU.mult, ALU.mult))
                v.tensor_tensor(by(h2, TT)[:, t, :], by(h2, TT)[:, t, :], sh2b, ALU.add) \
                    .then_inc(sem("h2_ready"), 1)
            dve.wait_ge(sem("router_mm"), 1)
            lg = psum[:, 2048:4096].rearrange("p (t n) -> p t n", t=TT)[:, :, 0:NE]
            mx = stat[:, 40:44]
            s(v.tensor_reduce(mx, lg, AX.X, ALU.max))
            v.tensor_tensor(by(affs, TT), lg, mx.unsqueeze(2).broadcast_to([P, TT, NE]), ALU.subtract) \
                .then_inc(sem("lg_ready"), 1)
            dve.sem_inc(sem("route_lg_done"), 1)
            dve.wait_ge(sem("aff_exp"), 1)
            s(v.tensor_reduce(stat[:, 44:48], by(affs, TT), AX.X, ALU.add))
            s(v.reciprocal(stat[:, 44:48], stat[:, 44:48]))
            v.tensor_tensor(by(aff, TT), by(affs, TT), stat[:, 44:48].unsqueeze(2).broadcast_to([P, TT, NE]),
                            ALU.mult).then_inc(sem("aff_ready"), 1)
            dve.wait_ge(sem("affT_ready"), 1)
            for r in range(SLOTS // 8):
                src = affT if r == 0 else work
                s(v.max(top8, src))
                s(v.match_replace(work, top8, src, -1.0))
            s(v.tensor_scalar(chosen, work, 0.0, None, ALU.is_lt))
            s(v.memset(work, 1.0))
            s(v.tensor_tensor_scan(count, work, chosen, 0.0, ALU.mult, ALU.add))
            s(v.tensor_tensor(count, count, chosen, ALU.mult))
            v.tensor_scalar(count, count, -1.0, None, ALU.add).then_inc(sem("rank_ready"), 1)
            dve.wait_ge(sem("rankT_mm"), 1)
            s(v.tensor_copy(rankT, bank(1)[:, 0:TT * NE]))
            s(v.memset(macc, 0.0))
            dve.sem_inc(sem("macc_ready"), 8)
            with dve.Fori(0, EPAIRS) as i:
                for e in range(2):
                    for t in range(TT):
                        ins = v.tensor_scalar(by(pick, TT)[:, t, e * SLOTS:(e + 1) * SLOTS], slot_row,
                                              rankT[:, bass.ds(2 * i + t * NE + e, 1)], None, ALU.is_equal)
                ins.then_inc(sem("pick_ready"), 1)
                dve.wait_ge(sem("pair_rows_in"), 64 * i + 64)
                v.scalar_tensor_tensor(put, rank_b, slot_col[:, 0:1], gate_b, ALU.is_equal, ALU.mult) \
                    .then_inc(sem("put_ready"), 1)
                for n in range(4):
                    c = slice(n * 512, (n + 1) * 512)
                    dve.wait_ge(sem("sig_ready"), 4 * i + n + 1)
                    v.tensor_tensor(hid[:, c], sig[:, c], bank(n), ALU.mult).then_inc(sem("silu_ready"), 1)
                dve.wait_ge(sem("ring_used"), PER_PAIR * i + 32)
                for n in range(4):
                    c = slice(n * 512, (n + 1) * 512)
                    dve.wait_ge(sem("silu_ready"), 4 * i + n + 1)
                    v.tensor_tensor(hid[:, c], hid[:, c], bank(4 + n), ALU.mult).then_inc(sem("hid_ready"), 1)
                for t in range(TT):
                    for n in range(2):
                        c = t * D + n * 512
                        dve.wait_ge(sem("put_mm"), 8 * i + 2 * t + n + 1)
                        v.tensor_tensor(macc[:, c:c + 512], macc[:, c:c + 512], bank((6 + 2 * t + n) % 8), ALU.add) \
                            .then_inc(sem("macc_ready"), 1)
            dve.wait_ge(sem("macc_ready"), 8 * EPAIRS + 8)
            dve.wait_ge(sem("gt2_in"), 16)
            for t in range(TT):
                s(v.tensor_tensor(by(macc, TT)[:, t, :], by(macc, TT)[:, t, :], gt2_keep, ALU.mult))
                v.tensor_tensor(by(x2, TT)[:, t, :], by(x2, TT)[:, t, :], by(macc, TT)[:, t, :], ALU.add) \
                    .then_inc(sem("x3_ready"), 1)
            dve.wait_ge(sem("x3_sq"), TT)
            s(rstd(None, "x3_ms", "x3_rms", 24))
            dve.wait_ge(sem("fin_in"), 16)
            dve.wait_ge(sem("xe_ready"), 2 * EPAIRS)
            for t in range(TT):
                v.scalar_tensor_tensor(by(h2, TT)[:, t, :], by(x2, TT)[:, t, :], stat[:, 36 + t:37 + t], fin_b,
                                       ALU.mult, ALU.mult).then_inc(sem("final_ready"), 1)


_INS = ["x", "c", "norm1_g", "norm2_g", "ada_w", "ada_b", "w_in", "attn_sink", "shift_mu", "decay_w0",
        "decay_w2", "iclr_a0", "iclr_a2", "gate_g2", "k_k", "k_a", "r_k", "lnx_g", "lnx_b", "w_br_attn",
        "w_br_rwkv", "w_out", "router_w", "exp_w_gate", "exp_w_up", "exp_w_down", "final_g"]


def kernel(**inputs):
    import numpy as _np
    import concourse.bacc as _bacc
    from concourse import mybir as _mybir
    from concourse.bass_utils import run_bass_kernel_spmd as _run

    nc = _bacc.Bacc("TRN2", target_bir_lowering=False, num_devices=1)
    arrays, args = {}, []
    for name in _INS:
        a = _np.ascontiguousarray(inputs[name])
        arrays[f"in_{name}_dram"] = a
        args.append(nc.dram_tensor(f"in_{name}_dram", a.shape, _mybir.dt.from_np(a.dtype), kind="ExternalInput").ap())
    args.append(nc.dram_tensor("out_dram", (1, T, D), F32, kind="ExternalOutput").ap())
    hybrid_layer(nc, *args)
    r = _run(nc, [arrays], core_ids=[0])
    return r.results[0]["out_dram"]
```

```python
from contextlib import ExitStack

import concourse.bass as bass
from concourse import mybir

P = 128
D, T = 1024, 512
KC = D // P
TT = T // P
HEADS, KV_HEADS, HD = 8, 2, 64
WINDOW = 128
RH, RN = 8, 64
CH = RH * RN
PAIRS = RH // 2
DIRS = 2
CHUNK = 64
STEPS = T // CHUNK
SUB = 16
LORA = 64
FEAT = 3 * CH + 2 * DIRS * LORA + 128
FB = FEAT // P
QB = HEADS * HD // P
RAWB = QB + 2 + FB
GATEB = 2 * D // P
GATE_COL = RAWB * P
NE, FF = 16, 2048
SLOTS = 2 * T // NE
EPAIRS = NE // 2
FBLK = FF // P
RING = 12
PER_PAIR = 2 * 24
GN_EPS, RMS_EPS = 64e-5, 1e-6
NEG = -1e30
KB = 256

ALU = mybir.AluOpType
ACT = mybir.ActivationFunctionType
AX = mybir.AxisListType
F32 = mybir.dt.float32

MU0, MU1, W0, A0, KKC, KAC, RKC, LG, LB, N1, CC = 0, 15, 30, 38, 46, 50, 54, 58, 62, 66, 74
NPAR = 82


class Signal:

    def __init__(self, sem):
        self.sem, self.n = sem, 0

    def step(self, eng, ins):
        self.n += 1
        ins.then_inc(self.sem, 1)
        eng.wait_ge(self.sem, self.n)


def hybrid_layer(nc, x, c, norm1_g, norm2_g, ada_w, ada_b, w_in, attn_sink, shift_mu, decay_w0,
                 decay_w2, iclr_a0, iclr_a2, gate_g2, k_k, k_a, r_k, lnx_g, lnx_b, w_br_attn,
                 w_br_rwkv, w_out, router_w, exp_w_gate, exp_w_up, exp_w_down, final_g, out):
    ctx = ExitStack()
    with ctx:
        def sb(name, cols, rows=P):
            return ctx.enter_context(nc.sbuf_tensor(name, [rows, cols], F32))[:, :]

        sems = {}

        def sem(name):
            if name not in sems:
                sems[name] = ctx.enter_context(nc.semaphore(name))
            return sems[name]

        mod_rows = nc.dram_tensor("mod_rows", (32, P), F32, kind="Internal").ap()
        gate_pre = nc.dram_tensor("gate_pre", (GATEB * P, T), F32, kind="Internal").ap()
        rank_rows = nc.dram_tensor("rank_rows", (NE, T), F32, kind="Internal").ap()
        gate_rows = nc.dram_tensor("gate_rows", (NE, T), F32, kind="Internal").ap()

        arena = sb("arena", 196 * KB)

        def at(kb, cols):
            return arena[:, int(kb * KB):int(kb * KB) + cols]

        ident = sb("ident", P)
        head_ones = sb("head_ones", P)
        mask_D = sb("mask_D", DIRS * P)
        mask_F = sb("mask_F", DIRS * P)
        mask_DT = sb("mask_DT", DIRS * P)
        mask_AT = sb("mask_AT", DIRS * P)
        mask_QT = sb("mask_QT", DIRS * CHUNK)
        same16 = sb("same16", P)
        half_sel = sb("half_sel", 2)
        neg_dist = sb("neg_dist", 3 * P)
        ones_col = sb("ones_col", 1)
        scan_keep = sb("scan_keep", T)
        slot_row = sb("slot_row", SLOTS)
        slot_col = sb("slot_col", 1)
        pcol = sb("pcol", NPAR)
        adab = sb("adab", 48)
        modT = sb("modT", 48)
        cond = sb("cond", KC)
        s1 = sb("s1", KC)
        mu_rest = sb("mu_rest", FB)
        one_minus_ka = sb("one_minus_ka", PAIRS)
        sinks = sb("sinks", HEADS)
        stat = sb("stat", 48)
        att_stat = sb("att_stat", 6 * HEADS)
        Pc = sb("Pc", STEPS * DIRS * PAIRS)

        LW, A_, KD, LC, E_ = (at(o, 16 * KB) for o in (0, 16, 32, 48, 64))
        hT = at(80, 16 * KB)
        attT, GG, BON = at(96, 8 * KB), at(104, 8 * KB), at(112, 8 * KB)
        Vt, Rt, Kt, KKt = at(120, 8 * KB), at(128, 8 * KB), at(136, 8 * KB), at(144, 8 * KB)
        X0 = 152
        x_in = LW
        raw = at(80 - 2 * RAWB, RAWB * T)
        ada_ring = [at(120 + 8 * s, 8 * KB) for s in range(4)]
        ada_acc = at(X0, 24 * KB)
        w_grp = [at(16, 16 * KB), at(96, 16 * KB)]
        par_rows, adab_rows, mod_rows_sb = at(X0 + 24, P), at(X0 + 25, P), at(X0 + 39, P)
        wd_t, ad_t, gd_t = (at(X0 + 24 + 2 * n, T) for n in range(3))
        w2_sb, a2_sb, g2_sb = (at(X0 + 30 + 2 * n, T) for n in range(3))
        kpad = at(X0, 2 * T)
        v_nat = at(X0 + 4, TT * P)
        p_all = at(X0 + 6, HEADS * 3 * P)
        pT = [at(X0 + 36, 3 * P), at(X0 + 37.5, 3 * P)]
        o_nat = at(X0 + 18, T)
        q_scaled = at(112, QB * T)
        w_gate_ring = [at(66, 8 * KB), at(172, 8 * KB), at(180, 8 * KB)]
        head_rk = at(X0 + 18, PAIRS * P)
        gate_stage = [at(74 + 2 * n, T) for n in range(3)]
        names = ["al_bd", "be_bd", "ka_bd", "v_bd", "be_nat", "ka_nat", "v_natp", "AkT", "Qs",
                 "D1", "D1T", "Fm", "Pt", "D2", "D2T"]
        place = {"al_bd": X0, "be_bd": X0 + 4, "ka_bd": X0 + 8, "v_bd": X0 + 12}
        free = [128, 132, 136, 140, 144, 148, X0 + 16, X0 + 20, X0 + 24, X0 + 28, X0 + 32]
        for n, o in zip(names[4:], free):
            place[n] = o
        tile = {n: at(o, 4 * KB) for n, o in place.items()}
        state = at(X0 + 36, 4 * KB)
        alrho = at(192, 4 * KB)
        tot_s = at(192, 32)
        yT = at(48, 16 * KB)

        def four(ap):
            return ap.rearrange("p (d m t) -> p d m t", d=DIRS, m=PAIRS)

        def bd(ap):
            return ap.rearrange("p (d m t) -> p d m t", d=DIRS, m=PAIRS)

        def by(ap, n):
            return ap.rearrange("p (n t) -> p n t", n=n)

        gates = at(128, 32 * KB)
        wba, wbr = at(80, 16 * KB), at(64, 16 * KB)
        wo = at(0, 32 * KB)
        rwT = at(32, 8 * KB)
        gn_tmp = at(40, 8 * KB)
        mixT = at(160, 16 * KB)
        ring = [at(8 * s, 8 * KB) for s in range(RING)]
        x2 = at(96, 16 * KB)
        h2 = at(112, 16 * KB)
        macc = at(128, 16 * KB)
        s2b, sh2b, gt1b, gt2b = (at(144 + 4 * n, D) for n in range(4))
        n2b = at(176, D)
        h2T = at(176, 16 * KB)
        sig = at(144, FF)
        gt2_keep = at(156, D)
        hid = at(160, FF)
        hidT = at(168, FBLK * P)
        xeT = at(176, KC * P)
        ye = at(180, D)
        pick = at(184, TT * 2 * SLOTS)
        rank_b, gate_b, put = at(186, T), at(188, T), at(190, T)
        fin_b = at(152, D)
        affT, work, chosen, count = (at(160 + 2 * n, T)[0:NE, :] for n in range(4))
        aff, affs = at(168, TT * NE), at(169, TT * NE)
        router_sb = at(140, KC * NE)
        top8 = sb("top8", 8, NE)
        rankT = sb("rankT", TT * NE)

        psum = ctx.enter_context(nc.psum_tensor("psum", [P, 8 * 512], F32))[:, :]

        def bank(b):
            return psum[:, b * 512:(b + 1) * 512]

        def gates_out(eng):
            for b in range(3):
                eng.wait_ge(sem(f"gate_out{b}"), 16 * len(range(b, GATEB, 3)))

        def mod_columns(pe, lo, hi):
            pe.wait_ge(sem("ada_used"), KC if hi <= 16 else 3 * KC)
            pe.wait_ge(sem("pcol_ready"), 2)
            for b in range(lo, hi):
                ins = nc.tensor.matmul(psum[:, 256 + b:257 + b], ada_acc[:, b * P:(b + 1) * P],
                                       ones_col[:, 0:1], start=True, stop=True)
            ins.then_inc(sem("mod_mm"), 1)

        def shifted(f):
            if f < 12:
                return by((Rt, Kt, Vt)[f // 4], 4)[:, f % 4, :]
            return (wd_t, ad_t, gd_t)[f - 12]

        products = {"A": 0, "B": 1, "C": 2, "Tbe": 3, "D2": 0, "D2T": 1, "Tka": 2, "Tv": 3, "P2": 0, "D4": 1,
                    "D4T": 2, "P4": 0, "D8": 1, "P8": 0, "G": 1, "W": 3, "U1": 0, "Ua": 1, "Ub": 0, "U": 1,
                    "Y": 2, "SU": 3}
        p_names = list(products)
        copies = ["be_nat", "D2", "D2T", "ka_nat", "v_nat", "D4", "D4T", "D8", "GT", "W", "U1"]
        vecs = ["D1", "DT", "F", "P1", "Qb", "AkT", "Qk", "P2", "P4", "P8", "Ua", "Ub", "U", "Ssum"]

        def scan_bank(name, d):
            return bank(2 * products[name] + d)

        def scan_made(eng, i, name, d):
            which, names = ("scan_copies", copies) if name in copies else ("scan_vecs", vecs)
            eng.wait_ge(sem(which), 2 * len(names) * i + 2 * names.index(name) + d + 1)

        def scan_product(eng, i, name, d):
            eng.wait_ge(sem("scan_mm"), 2 * len(p_names) * (i + 1) + 2 * p_names.index(name) + d + 1)

        block = ctx.enter_context(nc.Block())

        w_in_v = w_in[0].rearrange("(k p) n -> p k n", p=P)

        @block.sync
        def _(sp):
            load = lambda dst, src, s: sp.dma_start(dst, src).then_inc(sem(s), 16)
            rows = [(MU0, shift_mu[0].rearrange("d (m p) -> (d m) p", p=P)),
                    (W0, decay_w0[0].rearrange("d (m p) -> (d m) p", p=P)),
                    (A0, iclr_a0[0].rearrange("d (m p) -> (d m) p", p=P)),
                    (KKC, k_k.rearrange("l (m p) -> (l m) p", p=P)),
                    (KAC, k_a.rearrange("l (m p) -> (l m) p", p=P)),
                    (RKC, r_k[0].rearrange("(m a) k -> m (a k)", a=2)),
                    (LG, lnx_g.rearrange("l (m p) -> (l m) p", p=P)),
                    (LB, lnx_b.rearrange("l (m p) -> (l m) p", p=P)),
                    (N1, norm1_g.rearrange("l (m p) -> (l m) p", p=P)),
                    (CC, c.rearrange("l (m p) -> (l m) p", p=P))]
            for r, src in rows:
                load(par_rows[r:r + src.shape[0], :], src, "params_in")
            load(adab_rows[0:48, :], ada_b.rearrange("l (m p) -> (l m) p", p=P), "params_in")
            load(by(x_in, TT), x[0].rearrange("(t p) d -> p t d", p=P), "x_in")

            def ada_piece(n):
                if n >= 4:
                    sp.wait_ge(sem("ada_used"), n - 3)
                load(ada_ring[n % 4], ada_w[0, (n % KC) * P:(n % KC + 1) * P,
                                            (n // KC) * 2048:(n // KC + 1) * 2048], f"ada_in{n % 4}")

            for n in range(KC):
                ada_piece(n)
            for h in range(HEADS):
                col = (h % 4) * P + (h // 4) * HD
                load(by(w_grp[0], KC)[:, :, col:col + HD], w_in_v[:, :, h * HD:(h + 1) * HD], "w_grp0_in")
            load(by(w_grp[1], KC), w_in_v[:, :, 512:1024], "w_grp1_in")
            for n in range(KC, 3 * KC):
                ada_piece(n)
            sp.wait_ge(sem("w2_free"), 1)
            load(w2_sb, decay_w2[0].rearrange("d l c -> (d l) c"), "lora_in")
            load(a2_sb, iclr_a2[0].rearrange("d l c -> (d l) c"), "lora_in")
            load(g2_sb, gate_g2[0], "lora_in")
            load(sinks, attn_sink[0:1, :].partition_broadcast(P), "sinks_in")
            with sp.Fori(0, 2) as it:
                for b in range(2):
                    sp.wait_ge(sem("proj_mm"), 8 * it + 4 * b + 4)
                    load(by(w_grp[b], KC), w_in_v[:, :, bass.ds(1024 * it + 512 * b + 1024, 512)],
                         f"w_grp{b}_in")
            sp.wait_ge(sem("mod_rows_ready"), 1)
            load(mod_rows, mod_rows_sb[0:32, :], "mod_rows_out")
            sp.wait_ge(sem("shift_done"), FB)
            sp.wait_ge(sem("lora_mm"), 20)
            for g in range(GATEB // 2):
                if g >= 3:
                    sp.wait_ge(sem("gate_mm"), 2 * (g - 2))
                load(by(w_gate_ring[g % 3], KC), w_in_v[:, :, GATE_COL + 256 * g:GATE_COL + 256 * (g + 1)],
                     f"w_gate{g % 3}_in")
                for idx in ((2 * g - 6, 2 * g - 5) if g >= 3 else ()):
                    sp.wait_ge(sem("gate_raw"), idx + 1)
                    load(gate_pre[idx * P:(idx + 1) * P, :], gate_stage[idx % 3], f"gate_out{idx % 3}")
            for idx in range(GATEB - 6, GATEB):
                sp.wait_ge(sem("gate_raw"), idx + 1)
                load(gate_pre[idx * P:(idx + 1) * P, :], gate_stage[idx % 3], f"gate_out{idx % 3}")
            sp.wait_ge(sem("gate_mm"), GATEB)
            load(by(wba, 4), w_br_attn[0].rearrange("(k p) n -> p k n", p=P), "wba_in")
            gates_out(sp)
            sp.wait_ge(sem("scan_done"), 1)
            load(by(gates, GATEB), gate_pre.rearrange("(g p) t -> p g t", p=P), "gates_in")
            load(by(wbr, 4), w_br_rwkv[0].rearrange("(k p) n -> p k n", p=P), "wbr_in")
            load(by(wo, KC), w_out[0].rearrange("(k p) n -> p k n", p=P), "wo_in")
            load(n2b, norm2_g[0:1, :].partition_broadcast(P), "n2_in")

            def expert_chunk(i, j):
                kind, k, e = j // 16, (j % 16) // 2, j % 2
                if kind < 2:
                    w = exp_w_up if kind else exp_w_gate
                    src = w[0, bass.ds(2 * i + e, 1), k * P:(k + 1) * P, :].rearrange("o p n -> p (o n)")
                    load(ring[j % RING], src, f"ring{j % RING}_in")
                else:
                    src = exp_w_down[0, bass.ds(2 * i + e, 1), 2 * k * P:(2 * k + 2) * P, :] \
                        .rearrange("o (b p) n -> p (o b) n", p=P)
                    load(by(ring[j % RING], 2), src, f"ring{j % RING}_in")

            sp.wait_ge(sem("gn_done"), 1)
            for j in (6, 7):
                expert_chunk(0, j)
            sp.wait_ge(sem("mod_rows_out"), 16)
            sp.wait_ge(sem("mixT_ready"), KC)
            row = lambda n: mod_rows[8 * n:8 * n + 8, :].rearrange("(o a) b -> o (a b)", o=1).partition_broadcast(P)
            load(gt1b, row(0), "rows_in")
            load(by(x2, TT), x[0].rearrange("(t p) d -> p t d", p=P), "rows_in")
            load(sh2b, row(1), "rows_in")
            load(s2b, row(2), "rows_in")
            load(by(router_sb, KC), router_w[0].rearrange("(k p) e -> p k e", p=P), "rows_in")
            for j in (4, 5, 8, 9, 10, 11):
                expert_chunk(0, j)
            sp.wait_ge(sem("out_mm"), TT)
            for j in range(4):
                expert_chunk(0, j)
            sp.wait_ge(sem("x2_ready"), TT)
            sp.wait_ge(sem("h2_ready"), TT)
            load(gt2_keep, row(3), "gt2_in")
            load(fin_b, final_g[:].rearrange("(o n) -> o n", o=1).partition_broadcast(P), "fin_in")
            sp.wait_ge(sem("rank_ready"), 1)
            load(rank_rows, count, "route_out")
            load(gate_rows, affT, "route_out")
            sp.wait_ge(sem("route_out"), 32)

            def pair_rows(i):
                for e in range(2):
                    for dst, src in ((rank_b, rank_rows), (gate_b, gate_rows)):
                        load(dst[e * SLOTS:(e + 1) * SLOTS, :],
                             src[bass.ds(2 * i + e, 1), :].partition_broadcast(SLOTS), "pair_rows_in")

            sp.wait_ge(sem("route_lg_done"), 1)
            pair_rows(0)
            with sp.Fori(0, EPAIRS - 1) as i:
                for j in range(RING, PER_PAIR + RING):
                    if j == PER_PAIR:
                        sp.wait_ge(sem("put_ready"), i + 1)
                        sp.sem_inc(sem("ring_reloads"), 1)
                        pair_rows(i + 1)
                    sp.wait_ge(sem("ring_used"), PER_PAIR * i + (j - RING + 1))
                    sp.sem_inc(sem("ring_reloads"), 1)
                    expert_chunk(i + j // PER_PAIR, j % PER_PAIR)
            last = EPAIRS - 1
            for j in range(RING, PER_PAIR):
                sp.wait_ge(sem("ring_used"), PER_PAIR * last + (j - RING + 1))
                expert_chunk(last, j)
            for t in range(TT):
                sp.wait_ge(sem("final_ready"), t + 1)
                load(out[0, t * P:(t + 1) * P, :], by(h2, TT)[:, t, :], "final_out")
            sp.wait_ge(sem("final_out"), 16 * TT)

        @block.gpsimd
        def _(pool):
            order = Signal(sem("pool_order"))
            s = lambda ins: order.step(pool, ins)

            def select(o, i, pattern, base, cm, fill, op=ALU.is_ge):
                s(nc.gpsimd.affine_select(out=o, in_=i, compare_op=op, fill=fill, base=base,
                                          pattern=pattern, channel_multiplier=cm))

            s(nc.gpsimd.memset(ident, 0.0))
            select(ident, ident, [[-1, P]], 0, 1, 1.0, ALU.not_equal)
            pool.sem_inc(sem("ident_ready"), 1)
            s(nc.gpsimd.memset(ones_col, 1.0))
            s(nc.gpsimd.memset(head_ones, 0.0))
            for h in range(2):
                s(nc.gpsimd.memset(head_ones[h * 64:(h + 1) * 64, h * 64:(h + 1) * 64], 1.0))
            s(nc.gpsimd.memset(half_sel, 0.0))
            for h in range(2):
                s(nc.gpsimd.memset(half_sel[h * 64:(h + 1) * 64, h:h + 1], 1.0))
            s(nc.gpsimd.memset(same16, 1.0))
            v = by(same16, P // SUB)
            select(v, v, [[-SUB, P // SUB], [0, SUB]], 0, 1, 0.0)
            select(v, v, [[SUB, P // SUB], [0, SUB]], SUB - 1, -1, 0.0)
            for m in (mask_F, mask_AT):
                s(nc.gpsimd.memset(m, 0.0))
            s(nc.gpsimd.memset(mask_QT, 1.0))
            for h in range(2):
                r = slice(h * 64, (h + 1) * 64)
                for d in range(2):
                    low = mask_F[r, d * P + h * 64:d * P + (h + 1) * 64]
                    upp = mask_AT[r, d * P + h * 64:d * P + (h + 1) * 64]
                    inc = mask_QT[r, d * 64:(d + 1) * 64]
                    sign = 1 if d == 0 else -1
                    s(nc.gpsimd.memset(low, 1.0))
                    s(nc.gpsimd.memset(upp, 1.0))
                    select(low, low, [[-sign, 64]], -1, sign, 0.0)
                    select(upp, upp, [[sign, 64]], -1, -sign, 0.0)
                    select(inc, inc, [[sign, 64]], 0, -sign, 0.0)
            for d in range(2):
                q = slice(d * P, (d + 1) * P)
                s(nc.gpsimd.tensor_tensor(mask_D[:, q], mask_F[:, q], same16, ALU.mult))
                s(nc.gpsimd.tensor_tensor(mask_DT[:, q], mask_AT[:, q], same16, ALU.mult))
                s(nc.gpsimd.tensor_tensor(mask_F[:, q], mask_F[:, q], mask_D[:, q], ALU.subtract))
            s(nc.gpsimd.memset(scan_keep, 1.0))
            s(nc.gpsimd.memset(by(scan_keep, STEPS)[:, :, 0:1], 0.0))
            s(nc.gpsimd.iota(neg_dist, [[-1, 3 * P]], base=P, channel_multiplier=1,
                             allow_small_or_imprecise_dtypes=True))
            pool.sem_inc(sem("dist_ready"), 1)
            s(nc.gpsimd.iota(slot_row, [[1, SLOTS]], base=0, channel_multiplier=0,
                             allow_small_or_imprecise_dtypes=True))
            for h in range(2):
                s(nc.gpsimd.iota(slot_col[h * 64:(h + 1) * 64, :], [[0, 1]], base=0, channel_multiplier=1,
                                 allow_small_or_imprecise_dtypes=True))
            pool.wait_ge(sem("dist_abs"), 1)
            select(neg_dist, neg_dist, [[1, 3 * P]], 0, -1, NEG)
            select(neg_dist, neg_dist, [[-1, 3 * P]], 2 * P, 1, NEG)
            pool.sem_inc(sem("consts_ready"), 1)

            pool.wait_ge(sem("kk_raw"), 1)
            bon = at(X0 + 8, 8 * KB)
            s(nc.gpsimd.tensor_tensor(bon, KD[:, 0:2048], KD[:, 2048:4096], ALU.add))
            s(nc.gpsimd.tensor_tensor(bon, bon, Rt, ALU.mult))
            pool.sem_inc(sem("bonus_in"), 1)
            pool.wait_ge(sem("exp_lc"), 1)
            pool.wait_ge(sem("Pc_ready"), 1)
            for d in range(DIRS):
                h = slice(d * 2048, (d + 1) * 2048)
                s(nc.gpsimd.tensor_tensor(E_[:, h], E_[:, h], Rt, ALU.mult))
            pool.wait_ge(sem("exp_neg"), 1)
            s(nc.gpsimd.tensor_tensor(KD, KD, LC, ALU.mult))

            pool.wait_ge(sem("prep_done"), 1)
            halves = half_sel.unsqueeze(1).unsqueeze(3).broadcast_to([P, PAIRS, 2, CHUNK])
            token = lambda i, d: bass.ds(pool.snap(i * CHUNK if d == 0 else (STEPS - 1) * CHUNK - i * CHUNK), CHUNK)
            ar = alrho.rearrange("p (d m w t) -> p d m w t", d=DIRS, m=PAIRS, w=2)
            with pool.Fori(0, STEPS) as i:
                toks = [token(i, d) for d in range(DIRS)]

                def spread(n, one, d):
                    return nc.gpsimd.tensor_tensor(
                        bd(tile[n])[:, d].rearrange("p m (h t) -> p m h t", h=2),
                        one.unsqueeze(2).broadcast_to([P, PAIRS, 2, CHUNK]), halves, ALU.mult)

                for d in range(DIRS):
                    pool.wait_ge(sem("scan_mm"), 2 * len(p_names) * i + 2 * p_names.index("Tv") + d + 1)
                    pool.sem_inc(sem("steps_begun"), 1)
                    spread("be_bd", four(A_)[:, d, :, toks[d]], d)
                    spread("ka_bd", four(KD)[:, d, :, toks[d]], d)
                    spread("v_bd", by(Vt, PAIRS)[:, :, toks[d]], d)
                for d in range(DIRS):
                    pool.wait_ge(sem("scan_mm"), 2 * len(p_names) * i + 2 * p_names.index("W") + d + 1)
                    pool.sem_inc(sem("steps_begun"), 1)
                    spread("al_bd", four(LW)[:, d, :, toks[d]], d)
                    nc.gpsimd.tensor_copy(ar[:, d, :, 0, :], four(LW)[:, d, :, toks[d]])
                    nc.gpsimd.tensor_copy(ar[:, d, :, 1, :], four(E_)[:, d, :, toks[d]]) \
                        .then_inc(sem("operands_ready"), 1)

        @block.tensor
        def _(pe):
            mm = nc.tensor.matmul
            pe.wait_ge(sem("ident_ready"), 1)
            pe.wait_ge(sem("params_in"), 176)
            nc.tensor.transpose(psum[:, 0:NPAR], par_rows[0:NPAR, :], ident[0:NPAR, 0:NPAR]) \
                .then_inc(sem("params_T"), 1)
            nc.tensor.transpose(psum[:, 128:176], adab_rows[0:48, :], ident[0:48, 0:48]) \
                .then_inc(sem("params_T"), 1)
            pe.wait_ge(sem("xn_ready"), TT)
            for k in range(KC):
                if k == 7:
                    mod_columns(pe, 0, KC * 2)
                    pe.wait_ge(sem("proj_bank_free"), 1)
                for t in range(TT):
                    ins = nc.tensor.transpose(bank(k % 7 + 1)[:, t * P:(t + 1) * P],
                                              by(x_in, TT)[:, t, k * P:(k + 1) * P], ident)
                ins.then_inc(sem("xT"), 1)

            def project(dst_sem, grp, lhs, idx, mod8, free):
                pe.wait_ge(sem("proj_bank_free"), free)
                for k in range(KC):
                    ins = mm(bank(mod8), lhs(k), by(hT, KC)[:, k, :], start=(k == 0), stop=(k == KC - 1))
                ins.then_inc(sem(dst_sem), 1)

            def plain(g, j):
                return lambda k: by(w_grp[g], KC)[:, k, j * P:(j + 1) * P]

            pe.wait_ge(sem("proj_bank_free"), KC)
            pe.wait_ge(sem("w_grp0_in"), 16 * HEADS)
            for j in range(4):
                project("proj_mm", 0, plain(0, j), j, j, KC)
            with pe.Fori(0, 2) as it:
                for b in range(2):
                    g = 1 - b
                    pe.wait_ge(sem(f"w_grp{g}_in"), 16 * it + (16, 16 * HEADS + 16)[b])
                    for j in range(4):
                        project("proj_mm", g, plain(g, j), None, (4 + 4 * b + j) % 8, 8 * it + 4 + 4 * b + j + 1)
            pe.wait_ge(sem("w_grp1_in"), 48)
            project("proj_mm", 1, plain(1, 0), 20, 4, 21)

            pe.wait_ge(sem("proj_bank_free"), KC + RAWB)
            mod_columns(pe, 16, 48)
            pe.wait_ge(sem("modT_ready"), 2)
            nc.tensor.transpose(bank(1)[0:32, 0:P], modT[:, 16:48], ident).then_inc(sem("modR"), 1)

            pe.wait_ge(sem("lora_in"), 48)
            pe.wait_ge(sem("lora_x"), 3)
            n = 0
            for what in range(2):
                for m in range(PAIRS):
                    for d in range(DIRS):
                        if n >= 6:
                            pe.wait_ge(sem("lora_out"), n - 5)
                        r = slice(d * 64, (d + 1) * 64)
                        mm(bank(2 + n % 6), (w2_sb, a2_sb)[what][r, m * P:(m + 1) * P],
                           (wd_t, ad_t)[what][r, :], start=True, stop=True).then_inc(sem("lora_mm"), 1)
                        n += 1
            for m in range(PAIRS):
                pe.wait_ge(sem("lora_out"), n - 5)
                mm(bank(2 + n % 6), g2_sb[:, m * P:(m + 1) * P], gd_t, start=True, stop=True) \
                    .then_inc(sem("lora_mm"), 1)
                n += 1

            pe.wait_ge(sem("lora_out"), 20)
            pe.wait_ge(sem("mod_rows_ready"), 1)
            for t in range(TT):
                ins = nc.tensor.transpose(bank(7)[:, t * P:(t + 1) * P], by(raw, RAWB)[:, QB + 1, t * P:(t + 1) * P], ident)
            ins.then_inc(sem("vT"), 1)
            pe.wait_ge(sem("kpad_ready"), 3)

            def gate_products(lo, hi):
                for n in range(lo, hi):
                    idx, k = n // KC, n % KC
                    if k == 0:
                        if idx % 2 == 0:
                            pe.wait_ge(sem(f"w_gate{idx // 2 % 3}_in"), 16 * (idx // 6 + 1))
                        if idx >= 2:
                            pe.wait_ge(sem("gate_raw"), idx - 1)
                    ins = mm(bank(2 + idx % 2),
                             by(w_gate_ring[idx // 2 % 3], KC)[:, k, (idx % 2) * P:(idx % 2 + 1) * P],
                             by(hT, KC)[:, k, :], start=(k == 0), stop=(k == KC - 1))
                    if k == KC - 1:
                        ins.then_inc(sem("gate_mm"), 1)

            for q in range(TT):
                lo, hi = max(q - 1, 0), min(q + 2, TT)
                for h in range(HEADS):
                    n = q * HEADS + h
                    if n >= 2:
                        pe.wait_ge(sem("logits_ready"), n - 1)
                    mm(bank(n % 2)[:, 0:(hi - lo) * P], by(q_scaled, QB)[:, h % 4, q * P:(q + 1) * P],
                       by(kpad, 2)[:, h // 4, lo * P:hi * P], start=True, stop=True) \
                        .then_inc(sem("scores_mm"), 1)
                gate_products(32 * q, 32 * q + 8)

                def transpose_probs(h):
                    n = q * HEADS + h
                    pe.wait_ge(sem("probs_ready"), n + 1)
                    if n >= 2:
                        pe.wait_ge(sem("pT_ready"), n - 1)
                    for j in range(hi - lo):
                        ins = nc.tensor.transpose(bank(4 + n % 2)[:, j * P:(j + 1) * P],
                                                  p_all.rearrange("p (h t) -> p h t", h=HEADS)[:, h, j * P:(j + 1) * P], ident)
                    ins.then_inc(sem("pT_mm"), 1)

                transpose_probs(0)
                for h in range(HEADS):
                    n = q * HEADS + h
                    if h < HEADS - 1:
                        transpose_probs(h + 1)
                    gate_products(32 * q + 8 + 2 * h, 32 * q + 10 + 2 * h)
                    if h == 0 and q:
                        pe.wait_ge(sem("o_ready"), q)
                    pe.wait_ge(sem("pT_ready"), n + 1)
                    for j in range(hi - lo):
                        ins = mm(bank(6)[:, h * HD:(h + 1) * HD], pT[n % 2][:, j * P:(j + 1) * P],
                                 by(v_nat, TT)[:, lo + j, (h // 4) * HD:(h // 4 + 1) * HD],
                                 start=(j == 0), stop=(j == hi - lo - 1))
                    ins.then_inc(sem("pv_mm"), 1)
                gate_products(32 * q + 24, 32 * q + 32)
                pe.wait_ge(sem("o_ready"), q + 1)
                if q:
                    pe.wait_ge(sem("attT_ready"), q)
                for m in range(4):
                    ins = nc.tensor.transpose(bank(7)[:, m * P:(m + 1) * P], o_nat[:, m * P:(m + 1) * P], ident)
                ins.then_inc(sem("attT_mm"), 1)

            pe.wait_ge(sem("attT_ready"), TT)
            pe.wait_ge(sem("kk_sq"), 1)
            for m in range(PAIRS):
                mm(bank(m), head_ones, by(at(X0, 8 * KB), PAIRS)[:, m, :], start=True, stop=True) \
                    .then_inc(sem("kk_mm"), 1)
            pe.wait_ge(sem("bonus_in"), 2)
            for m in range(PAIRS):
                mm(bank(4 + m), head_rk[:, m * P:(m + 1) * P], by(at(X0 + 8, 8 * KB), PAIRS)[:, m, :], start=True, stop=True) \
                    .then_inc(sem("bonus_mm"), 1)

            B = {n: bd(t) for n, t in tile.items()}
            S_bd = bd(state)
            ar = alrho.rearrange("p (d m x) -> p d m x", d=DIRS, m=PAIRS)
            Q = tile["Qs"].rearrange("p (d w m t) -> p w d m t", w=2, d=DIRS, m=PAIRS)
            pe.sem_inc(sem("scan_mm"), 2 * len(p_names))
            with pe.Fori(0, STEPS) as i:
                def product(name, waits, terms, width=P, signal=True, first=True, last=True):
                    for d in range(DIRS):
                        for w in waits:
                            if w in ("operands_ready", "y_free", "state_ready"):
                                pe.wait_ge(sem(w), 2 * i + d + 1)
                            else:
                                scan_made(pe, i, w, d)
                        for m in range(PAIRS):
                            o = scan_bank(name, d)[:, m * width:(m + 1) * width]
                            for a, (lt, rh) in enumerate(terms):
                                ins = mm(o, lt(d, m), rh(d, m), start=(first and a == 0 and (last or m == 0)),
                                         stop=(last and a == len(terms) - 1 and (first or m == PAIRS - 1)))
                        if signal:
                            ins.then_inc(sem("scan_mm"), 1)

                def transposed(name, waits, src):
                    for d in range(DIRS):
                        for w in waits:
                            scan_made(pe, i, w, d) if w != "state_ready" else pe.wait_ge(sem(w), 2 * i + d + 1)
                        for m in range(PAIRS):
                            ins = nc.tensor.transpose(scan_bank(name, d)[:, m * P:(m + 1) * P],
                                                      B[src][:, d, m, :], ident)
                        ins.then_inc(sem("scan_mm"), 1)

                def t_(n):
                    return lambda d, m: B[n][:, d, m, :]

                alpha_rho, St = (lambda d, m: ar[:, d, m, :]), (lambda d, m: S_bd[:, d, m, :])
                product("A", ["operands_ready"], [(t_("al_bd"), t_("be_bd"))])
                product("B", [], [(t_("be_bd"), alpha_rho)])
                product("C", ["y_free"], [(t_("ka_bd"), alpha_rho)])
                transposed("Tbe", ["state_ready"], "be_bd")
                product("D2", ["D1", "DT", "F"], [(t_("D1T"), t_("D1"))])
                product("D2T", ["Qb"], [(t_("D1"), t_("D1T"))])
                transposed("Tka", ["AkT", "Qk"], "ka_bd")
                transposed("Tv", ["be_nat"], "v_bd")
                product("P2", ["D2", "P1"], [(t_("D2"), t_("Pt"))])
                product("D4", ["D2T"], [(t_("D2T"), t_("D2"))])
                product("D4T", ["ka_nat"], [(t_("D2"), t_("D2T"))])
                product("W", ["v_nat"], [(t_("AkT"), t_("v_natp"))], signal=False, last=False)
                product("P4", ["D4", "P2"], [(t_("D1"), t_("Pt"))])
                product("D8", ["D4T"], [(t_("D1T"), t_("D1"))])
                product("Y", [], [(t_("v_natp"), lambda d, m: Q[:, 1, d, m, :])], width=CHUNK,
                        signal=False, last=False)
                product("P8", ["D8", "P4"], [(t_("D2"), t_("Pt"))])
                product("Y", [], [(St, lambda d, m: ar[:, d, m, CHUNK:2 * CHUNK])], width=CHUNK,
                        signal=False, first=False, last=False)
                product("G", ["P8"], [(t_("Fm"), t_("Pt"))])
                product("W", [], [(t_("al_bd"), St)], first=False)
                product("U1", ["W"], [(t_("Pt"), t_("Fm"))])
                product("Ua", ["U1", "GT"], [(t_("D2T"), t_("D1T"))])
                product("Ub", ["Ua"], [(t_("D2T"), t_("D1"))])
                product("U", ["Ub"], [(t_("D2T"), t_("D2"))])
                product("Y", ["U"], [(t_("Fm"), lambda d, m: Q[:, 0, d, m, :])], width=CHUNK, first=False)
                product("SU", [], [(t_("be_nat"), t_("Fm")), (t_("ka_nat"), t_("v_natp"))])

            pe.wait_ge(sem("y_sum"), 1)
            for m in range(PAIRS):
                mm(bank(m), head_ones, by(yT[:, 0:8 * KB], PAIRS)[:, m, :], start=True, stop=True) \
                    .then_inc(sem("gn_mean_mm"), 1)
            pe.wait_ge(sem("gn_sq"), 1)
            for m in range(PAIRS):
                mm(bank(4 + m), head_ones, by(yT[:, 8 * KB:16 * KB], PAIRS)[:, m, :], start=True, stop=True) \
                    .then_inc(sem("gn_var_mm"), 1)

            def branch(w, src, b, m):
                for k in range(4):
                    ins = mm(bank(b), by(w, 4)[:, k, m * P:(m + 1) * P], by(src, 4)[:, k, :],
                             start=(k == 0), stop=(k == 3))
                return ins

            pe.wait_ge(sem("gn_centred"), 1)
            pe.wait_ge(sem("wba_in"), 16)
            for m in range(4):
                branch(wba, attT, m, m)
            pe.wait_ge(sem("wbr_in"), 16)
            pe.wait_ge(sem("gn_vare"), PAIRS)
            pe.wait_ge(sem("rwT_ready"), 1)
            for m in range(KC):
                if m >= 4:
                    pe.wait_ge(sem("mixT_ready"), m - 3)
                    branch(wba, attT, m % 4, m)
                branch(wbr, rwT, 4 + m % 4, m).then_inc(sem("mix_mm"), 1)
            pe.wait_ge(sem("wo_in"), 16)
            pe.wait_ge(sem("mixT_ready"), KC)
            def out_proj(t):
                for n in range(2):
                    for k in range(KC):
                        ins = mm(bank(2 * t + n), by(mixT, KC)[:, k, t * P:(t + 1) * P],
                                 by(wo, KC)[:, k, n * 512:(n + 1) * 512], start=(k == 0), stop=(k == KC - 1))
                ins.then_inc(sem("out_mm"), 1)

            def h2_transposed(t):
                pe.wait_ge(sem("h2_ready"), t + 1)
                for k in range(KC):
                    ins = nc.tensor.transpose(bank(2 * t + k // 4)[:, (k % 4) * P:(k % 4 + 1) * P],
                                              by(h2, TT)[:, t, k * P:(k + 1) * P], ident)
                ins.then_inc(sem("h2T_mm"), 1)

            def router(t):
                pe.wait_ge(sem("h2T_ready"), t + 1)
                for k in range(KC):
                    ins = mm(bank(2 * t)[:, 0:NE], by(h2T, KC)[:, k, t * P:(t + 1) * P],
                             by(router_sb, KC)[:, k, :], start=(k == 0), stop=(k == KC - 1))
                ins.then_inc(sem("router_mm"), 1)

            out_proj(0)
            out_proj(1)
            pe.wait_ge(sem("rows_in"), 80)
            h2_transposed(0)
            out_proj(2)
            router(0)
            h2_transposed(1)
            out_proj(3)
            router(1)
            h2_transposed(2)
            router(2)
            h2_transposed(3)
            router(3)
            pe.wait_ge(sem("aff_ready"), 1)
            for t in range(TT):
                ins = nc.tensor.transpose(bank(0)[0:NE, t * P:(t + 1) * P], by(aff, TT)[:, t, :], ident)
            ins.then_inc(sem("affT_mm"), 1)
            pe.wait_ge(sem("rank_ready"), 1)
            for t in range(TT):
                ins = nc.tensor.transpose(bank(1)[:, t * NE:(t + 1) * NE], count[:, t * P:(t + 1) * P],
                                          ident[0:NE, 0:NE])
            ins.then_inc(sem("rankT_mm"), 1)

            with pe.Fori(0, EPAIRS) as i:
                pe.wait_ge(sem("pick_ready"), i + 1)
                pe.wait_ge(sem("macc_ready"), 8 * i + 8)
                for k in range(KC):
                    for t in range(TT):
                        ins = mm(bank(k // 4)[:, (k % 4) * P:(k % 4 + 1) * P],
                                 by(h2, TT)[:, t, k * P:(k + 1) * P], by(pick, TT)[:, t, :],
                                 start=(t == 0), stop=(t == TT - 1))
                    if k % 4 == 3:
                        ins.then_inc(sem("xe_mm"), 1)
                pe.wait_ge(sem("xe_ready"), 2 * i + 2)
                for j in range(32):
                    kind, k, e = j // 16, (j % 16) // 2, j % 2
                    pe.wait_ge(sem(f"ring{j % RING}_in"), 64 * i + 16 * (j // RING + 1))
                    for n in range(4):
                        ins = mm(bank(4 * kind + n)[e * 64:(e + 1) * 64, :],
                                 by(xeT, KC)[:, k, e * 64:(e + 1) * 64],
                                 ring[j % RING][:, n * 512:(n + 1) * 512],
                                 start=(k == 0), stop=(k == KC - 1))
                    ins.then_inc(sem("ring_used"), 1)
                for n in range(4):
                    pe.wait_ge(sem("hid_ready"), 4 * i + n + 1)
                    for f in range(4):
                        ins = nc.tensor.transpose(bank(n)[:, f * P:(f + 1) * P],
                                                  hid[:, (4 * n + f) * P:(4 * n + f + 1) * P], ident)
                    ins.then_inc(sem("hidT_mm"), 1)
                for j in range(32, 48):
                    k, e = (j % 16) // 2, j % 2
                    pe.wait_ge(sem(f"ring{j % RING}_in"), 64 * i + 16 * (j // RING + 1))
                    if e == 0 and k % 2 == 0:
                        pe.wait_ge(sem("hidT_ready"), 4 * i + k // 2 + 1)
                    for b in range(2):
                        for n in range(2):
                            ins = mm(bank(4 + n)[e * 64:(e + 1) * 64, :],
                                     by(hidT, FBLK)[:, 2 * k + b, e * 64:(e + 1) * 64],
                                     by(ring[j % RING], 2)[:, b, n * 512:(n + 1) * 512],
                                     start=(k == 0 and b == 0), stop=(k == 7 and b == 1))
                    ins.then_inc(sem("ring_used"), 1)
                pe.wait_ge(sem("ye_ready"), i + 1)
                pe.wait_ge(sem("put_ready"), i + 1)
                for t in range(TT):
                    for n in range(2):
                        mm(bank((6 + 2 * t + n) % 8), put[:, t * P:(t + 1) * P], ye[:, n * 512:(n + 1) * 512],
                           start=True, stop=True).then_inc(sem("put_mm"), 1)

        @block.scalar
        def _(act):
            order = Signal(sem("act_order"))
            fn = nc.scalar.activation
            act.wait_ge(sem("pcol_ready"), 1)
            fn(stat[:, 0:KC], pcol[:, CC:CC + KC], ACT.Sigmoid).then_inc(sem("sig_c"), 1)
            act.wait_ge(sem("x_in"), 16)
            for t in range(TT):
                ins = fn(at(112, D), by(x_in, TT)[:, t, :], ACT.Square, accum_out=stat[:, 8 + t:9 + t])
                order.step(act, ins)
            act.sem_inc(sem("x_sq"), 1)
            act.wait_ge(sem("x_ms"), 1)
            fn(stat[:, 16:20], stat[:, 12:16], ACT.Sqrt).then_inc(sem("x_rms"), 1)
            act.wait_ge(sem("x_rstd"), 1)
            for t in range(TT):
                fn(by(x_in, TT)[:, t, :], by(x_in, TT)[:, t, :], ACT.Copy, scale=stat[:, 20 + t:21 + t]) \
                    .then_inc(sem("xn_ready"), 1)

            rawb = by(raw, RAWB)
            for idx in range(4):
                act.wait_ge(sem("proj_mm"), idx + 1)
                fn(rawb[:, idx, :], bank(idx), ACT.Copy).then_inc(sem("proj_bank_free"), 1)
            with act.Fori(0, 2) as it:
                for j in range(8):
                    act.wait_ge(sem("proj_mm"), 8 * it + 4 + j + 1)
                    fn(raw[:, bass.ds(8 * T * it + (4 + j) * T, T)], bank((4 + j) % 8), ACT.Copy) \
                        .then_inc(sem("proj_bank_free"), 1)
            act.wait_ge(sem("proj_mm"), 21)
            fn(rawb[:, 20, :], bank(4), ACT.Copy).then_inc(sem("proj_bank_free"), 1)
            act.wait_ge(sem("shift_done"), FB)
            fn(wd_t, wd_t, ACT.Tanh).then_inc(sem("lora_x"), 1)
            fn(gd_t, gd_t, ACT.Sigmoid).then_inc(sem("lora_x"), 1)
            act.sem_inc(sem("lora_x"), 1)
            n = 0
            for what in range(2):
                for m in range(PAIRS):
                    for d in range(DIRS):
                        act.wait_ge(sem("lora_mm"), n + 1)
                        col = (W0, A0)[what] + 4 * d + m
                        fn(four((LW, A_)[what])[:, d, m, :], bank(2 + n % 6), ACT.Sigmoid,
                           bias=pcol[:, col:col + 1]).then_inc(sem("lora_out"), 1)
                        n += 1
            for m in range(PAIRS):
                act.wait_ge(sem("lora_mm"), n + 1)
                fn(by(GG, PAIRS)[:, m, :], bank(2 + n % 6), ACT.Copy).then_inc(sem("lora_out"), 1)
                n += 1
            pv = p_all.rearrange("p (h t) -> p h t", h=HEADS)
            ast = by(att_stat, 6)

            def gate_out(idx):
                act.wait_ge(sem("gate_mm"), idx + 1)
                if idx >= 3:
                    act.wait_ge(sem(f"gate_out{idx % 3}"), 16 * (idx // 3))
                fn(gate_stage[idx % 3], bank(2 + idx % 2), ACT.Copy).then_inc(sem("gate_raw"), 1)

            act.wait_ge(sem("lora_mm"), 20)
            for q in range(TT):
                nk = min(q + 2, TT) - max(q - 1, 0)
                act.wait_ge(sem("att_max"), q + 1)
                fn(ast[:, 3, :], ast[:, 2, :], ACT.Exp).then_inc(sem("sink_exp"), 1)
                for h in range(HEADS):
                    fn(pv[:, h, 0:nk * P], pv[:, h, 0:nk * P], ACT.Exp, bias=ast[:, 1, h:h + 1],
                       accum_out=ast[:, 4, h:h + 1]).then_inc(sem("probs_ready"), 1)
                    if h == 2:
                        gate_out(4 * q)
                for idx in range(4 * q + 1, 4 * q + 4):
                    gate_out(idx)
                act.wait_ge(sem("attT_mm"), q + 1)
                fn(by(attT, 4)[:, :, q * P:(q + 1) * P], by(bank(7), 4), ACT.Copy) \
                    .then_inc(sem("attT_ready"), 1)
            act.wait_ge(sem("kk_raw"), 1)
            fn(at(X0, 8 * KB), KKt, ACT.Square).then_inc(sem("kk_sq"), 1)
            for m in range(PAIRS):
                act.wait_ge(sem("kk_mm"), m + 1)
                fn(by(at(X0, 8 * KB), PAIRS)[:, m, :], bank(m), ACT.Sqrt).then_inc(sem("kk_norm"), 1)
            gates_out(act)
            fn(E_, LC, ACT.Exp).then_inc(sem("exp_lc"), 1)
            fn(LW, LW, ACT.Exp).then_inc(sem("exp_lcw"), 1)
            act.wait_ge(sem("exp_lc"), 1)
            fn(LC, LC, ACT.Exp, scale=-1.0).then_inc(sem("exp_neg"), 1)

            act.sem_inc(sem("y_free"), 2)
            yv = four(yT)
            B = {n: bd(t) for n, t in tile.items()}

            with act.Fori(0, STEPS) as i:
                def copy_out(name, dst):
                    for d in range(DIRS):
                        scan_product(act, i, name, d)
                        fn(B[dst][:, d], by(scan_bank(name, d), PAIRS), ACT.Copy).then_inc(sem("scan_copies"), 1)

                copy_out("Tbe", "be_nat")
                copy_out("D2", "D2")
                copy_out("D2T", "D2T")
                copy_out("Tka", "ka_nat")
                copy_out("Tv", "v_natp")
                copy_out("D4", "D1")
                copy_out("D4T", "D1T")
                copy_out("D8", "D2")
                copy_out("G", "D2T")
                copy_out("W", "Fm")
                copy_out("U1", "D1T")
                for d in range(DIRS):
                    tok = bass.ds(i * CHUNK if d == 0 else (STEPS - 1) * CHUNK - i * CHUNK, CHUNK)
                    scan_product(act, i, "Y", d)
                    fn(yv[:, d, :, tok], by(scan_bank("Y", d)[:, 0:PAIRS * CHUNK], PAIRS), ACT.Copy) \
                        .then_inc(sem("y_free"), 1)

            act.wait_ge(sem("gn_centred"), 1)
            fn(yT[:, 8 * KB:16 * KB], yT[:, 0:8 * KB], ACT.Square).then_inc(sem("gn_sq"), 1)
            act.wait_ge(sem("gn_vare"), 4)
            fn(gn_tmp, gn_tmp, ACT.Sqrt).then_inc(sem("gn_std"), 1)
            act.wait_ge(sem("gates_in"), 16)
            for n in range(4):
                g = gates[:, n * 2048:(n + 1) * 2048]
                fn(g, g, ACT.Sigmoid).then_inc(sem("gate_ready"), 1)
            def h2_out(t):
                act.wait_ge(sem("h2T_mm"), t + 1)
                fn(by(h2T, KC)[:, :, t * P:(t + 1) * P], by(psum[:, 1024 * t:1024 * (t + 1)], KC), ACT.Copy) \
                    .then_inc(sem("h2T_ready"), 1)

            for t in range(TT):
                act.wait_ge(sem("x2_ready"), t + 1)
                if t:
                    act.wait_ge(sem("x2_sq"), t)
                fn(at(132, D), by(x2, TT)[:, t, :], ACT.Square, accum_out=stat[:, 8 + t:9 + t]) \
                    .then_inc(sem("x2_sq"), 1)
                act.wait_ge(sem("x2_ms"), t + 1)
                fn(stat[:, 16 + t:17 + t], stat[:, 12 + t:13 + t], ACT.Sqrt).then_inc(sem("x2_rms"), 1)
                if t:
                    h2_out(t - 1)
            h2_out(TT - 1)
            act.wait_ge(sem("lg_ready"), 1)
            fn(affs, affs, ACT.Exp).then_inc(sem("aff_exp"), 1)
            act.wait_ge(sem("affT_mm"), 1)
            fn(affT, bank(0)[0:NE, :], ACT.Copy).then_inc(sem("affT_ready"), 1)
            with act.Fori(0, EPAIRS) as i:
                for g in range(2):
                    act.wait_ge(sem("xe_mm"), 2 * i + g + 1)
                    fn(xeT[:, g * 512:(g + 1) * 512], bank(g), ACT.Copy).then_inc(sem("xe_ready"), 1)
                act.wait_ge(sem("ring_used"), PER_PAIR * i + 16)
                for n in range(4):
                    fn(sig[:, n * 512:(n + 1) * 512], bank(n), ACT.Sigmoid).then_inc(sem("sig_ready"), 1)
                for n in range(4):
                    act.wait_ge(sem("hidT_mm"), 4 * i + n + 1)
                    fn(hidT[:, n * 512:(n + 1) * 512], bank(n), ACT.Copy).then_inc(sem("hidT_ready"), 1)
                act.wait_ge(sem("ring_used"), PER_PAIR * i + PER_PAIR)
                fn(ye, psum[:, 4 * 512:6 * 512], ACT.Copy).then_inc(sem("ye_ready"), 1)
            for t in range(TT):
                act.wait_ge(sem("x3_ready"), t + 1)
                fn(at(160, D), by(x2, TT)[:, t, :], ACT.Square, accum_out=stat[:, 24 + t:25 + t]) \
                    .then_inc(sem("x3_sq"), 1)
                act.wait_ge(sem("x3_sq"), t + 1)
            act.wait_ge(sem("x3_ms"), 1)
            fn(stat[:, 32:36], stat[:, 28:32], ACT.Sqrt).then_inc(sem("x3_rms"), 1)

        @block.vector
        def _(dve):
            v = nc.vector
            order = Signal(sem("dve_order"))
            s = lambda ins: order.step(dve, ins)
            dve.wait_ge(sem("params_T"), 2)
            v.tensor_copy(pcol, psum[:, 0:NPAR]).then_inc(sem("pcol_ready"), 1)
            v.tensor_copy(adab, psum[:, 128:176]).then_inc(sem("pcol_ready"), 1)
            dve.wait_ge(sem("pcol_ready"), 2)
            s(v.tensor_tensor(mu_rest, pcol[:, MU0:MU0 + FB], pcol[:, MU1:MU1 + FB], ALU.add))
            s(v.tensor_scalar(mu_rest, mu_rest, -1.0, 1.0, ALU.mult, ALU.add))
            s(v.tensor_scalar(one_minus_ka, pcol[:, KAC:KAC + 4], -1.0, 1.0, ALU.mult, ALU.add))
            dve.wait_ge(sem("sig_c"), 1)
            s(v.tensor_tensor(cond, pcol[:, CC:CC + KC], stat[:, 0:KC], ALU.mult))
            dve.wait_ge(sem("dist_ready"), 1)
            dist_tmp = at(116, 3 * P)
            s(v.tensor_scalar(dist_tmp, neg_dist, -1.0, None, ALU.mult))
            v.tensor_tensor(dist_tmp, dist_tmp, neg_dist, ALU.min).then_inc(sem("dist_min"), 1)

            def ada(n):
                dve.wait_ge(sem(f"ada_in{n % 4}"), 16 * (n // 4 + 1))
                k, part = n % KC, ada_acc[:, (n // KC) * 2048:(n // KC + 1) * 2048]
                if k == 0:
                    ins = v.tensor_scalar(part, ada_ring[n % 4], cond[:, 0:1], None, ALU.mult)
                else:
                    dve.wait_ge(sem("ada_used"), n)
                    ins = v.scalar_tensor_tensor(part, ada_ring[n % 4], cond[:, k:k + 1], part, ALU.mult, ALU.add)
                ins.then_inc(sem("ada_used"), 1)

            def rstd(src, ms_sem, rms_sem, base):
                v.tensor_scalar(stat[:, base + 4:base + 8], stat[:, base:base + 4], 1.0 / D, RMS_EPS,
                                ALU.mult, ALU.add).then_inc(sem(ms_sem), 1)
                dve.wait_ge(sem(rms_sem), 1)
                return v.reciprocal(stat[:, base + 12:base + 16], stat[:, base + 8:base + 12])

            dve.wait_ge(sem("dist_min"), 1)
            v.tensor_copy(neg_dist, dist_tmp).then_inc(sem("dist_abs"), 1)
            dve.wait_ge(sem("x_sq"), 1)
            rstd(None, "x_ms", "x_rms", 8).then_inc(sem("x_rstd"), 1)
            for n in range(KC):
                ada(n)
            dve.wait_ge(sem("mod_mm"), 1)
            v.tensor_tensor(modT[:, 0:16], psum[:, 256:272], adab[:, 0:16], ALU.add).then_inc(sem("modT_ready"), 1)
            dve.wait_ge(sem("modT_ready"), 1)
            s(v.tensor_scalar(s1, modT[:, KC:2 * KC], 1.0, None, ALU.add))
            s(v.tensor_tensor(s1, s1, pcol[:, N1:N1 + KC], ALU.mult))
            for k in range(KC):
                dve.wait_ge(sem("xT"), k + 1)
                v.tensor_scalar(by(hT, KC)[:, k, :], bank(k % 7 + 1), s1[:, k:k + 1], modT[:, k:k + 1],
                                ALU.mult, ALU.add).then_inc(sem("proj_bank_free"), 1)
            for n in range(KC, 3 * KC):
                ada(n)
            dve.sem_inc(sem("w2_free"), 1)
            dve.wait_ge(sem("ada_used"), 3 * KC)
            rawb = by(raw, RAWB)
            for f in range(FB):
                dve.wait_ge(sem("proj_bank_free"), KC + QB + 2 + f + 1)
                p = rawb[:, QB + 2 + f, :]
                o = shifted(f)
                s(v.tensor_scalar(o, p, mu_rest[:, f:f + 1], None, ALU.mult))
                s(v.scalar_tensor_tensor(o[:, 1:T], p[:, 0:T - 1], pcol[:, MU0 + f:MU0 + f + 1], o[:, 1:T],
                                         ALU.mult, ALU.add))
                v.scalar_tensor_tensor(o[:, 0:T - 1], p[:, 1:T], pcol[:, MU1 + f:MU1 + f + 1], o[:, 0:T - 1],
                                       ALU.mult, ALU.add).then_inc(sem("shift_done"), 1)
            dve.wait_ge(sem("mod_mm"), 2)
            v.tensor_tensor(modT[:, 16:48], psum[:, 272:304], adab[:, 16:48], ALU.add) \
                .then_inc(sem("modT_ready"), 1)
            dve.wait_ge(sem("modR"), 1)
            v.tensor_copy(mod_rows_sb[0:32, :], bank(1)[0:32, 0:P]).then_inc(sem("mod_rows_ready"), 1)

            dve.wait_ge(sem("mod_mm"), 2)
            q_all = raw[:, 0:QB * T]
            v.tensor_scalar(q_scaled, q_all, HD ** -0.5, None, ALU.mult).then_inc(sem("kpad_ready"), 1)
            dve.wait_ge(sem("consts_ready"), 1)
            for h in range(2):
                ins = v.tensor_scalar(by(kpad, 2)[:, h, :], rawb[:, QB, :], half_sel[:, h:h + 1], None, ALU.mult)
            ins.then_inc(sem("kpad_ready"), 1)
            dve.wait_ge(sem("vT"), 1)
            v.tensor_copy(v_nat, bank(7)).then_inc(sem("kpad_ready"), 1)
            dve.wait_ge(sem("sinks_in"), 16)
            pv = p_all.rearrange("p (h t) -> p h t", h=HEADS)

            def prepare(part, n):
                d, m = n // 4, n % 4
                lw, lc, kd = (four(a)[:, d, m, :] for a in (LW, LC, KD))
                if part == 0:
                    if d == 0:
                        s(v.tensor_scalar(by(KKt, 4)[:, m, :], by(Kt, 4)[:, m, :], pcol[:, KKC + m:KKC + m + 1],
                                          None, ALU.mult))
                    s(v.tensor_scalar(lw, lw, -float(2.718281828459045 ** -0.5), None, ALU.mult))
                elif part == 1:
                    s(v.tensor_scalar(kd, four(A_)[:, d, m, :], pcol[:, KAC + m:KAC + m + 1],
                                      one_minus_ka[:, m:m + 1], ALU.mult, ALU.add))
                    s(v.tensor_tensor(kd, kd, by(Kt, 4)[:, m, :], ALU.mult))
                elif part == 2:
                    s(v.tensor_tensor_scan(lc, scan_keep, lw, 0.0, ALU.mult, ALU.add))
                    if d == 1:
                        back, tot = by(lc, STEPS), tot_s[:, 0:STEPS].unsqueeze(2)
                        s(v.tensor_copy(tot, back[:, :, CHUNK - 1:CHUNK]))
                        s(v.tensor_tensor(back, tot.broadcast_to([P, STEPS, CHUNK]), back, ALU.subtract))
                        s(v.tensor_tensor(lc, lc, lw, ALU.add))
                else:
                    s(v.tensor_tensor(lw, lc, lw, ALU.subtract))

            dve.wait_ge(sem("lora_out"), 20)
            ast = by(att_stat, 6)
            for q in range(TT):
                lo, hi = max(q - 1, 0), min(q + 2, TT)
                w = (hi - lo) * P
                band = slice((lo - q + 1) * P, (hi - q + 1) * P)
                if q:
                    dve.wait_ge(sem("pT_mm"), HEADS * q)
                for h in range(HEADS):
                    dve.wait_ge(sem("scores_mm"), q * HEADS + h + 1)
                    v.scalar_tensor_tensor(pv[:, h, 0:w], neg_dist[:, band], 2.0 ** -(h + 1),
                                           bank((q * HEADS + h) % 2)[:, 0:w], ALU.mult, ALU.add) \
                        .then_inc(sem("logits_ready"), 1)
                dve.wait_ge(sem("logits_ready"), HEADS * (q + 1))
                s(v.tensor_reduce(ast[:, 0, :], pv[:, :, 0:w], AX.X, ALU.max))
                s(v.tensor_tensor(ast[:, 0, :], ast[:, 0, :], sinks, ALU.max))
                s(v.tensor_tensor(ast[:, 2, :], sinks, ast[:, 0, :], ALU.subtract))
                v.tensor_scalar(ast[:, 1, :], ast[:, 0, :], -1.0, None, ALU.mult).then_inc(sem("att_max"), 1)
                for h in range(HEADS):
                    n = q * HEADS + h
                    dve.wait_ge(sem("pT_mm"), n + 1)
                    if n >= 2:
                        dve.wait_ge(sem("pv_mm"), n - 1)
                    v.tensor_copy(pT[n % 2][:, 0:w], bank(4 + n % 2)[:, 0:w]).then_inc(sem("pT_ready"), 1)
                    prepare(n // 8, n % 8)
                dve.wait_ge(sem("sink_exp"), q + 1)
                dve.wait_ge(sem("probs_ready"), HEADS * (q + 1))
                s(v.tensor_tensor(ast[:, 5, :], ast[:, 4, :], ast[:, 3, :], ALU.add))
                s(v.reciprocal(ast[:, 5, :], ast[:, 5, :]))
                dve.wait_ge(sem("pv_mm"), HEADS * (q + 1))
                if q:
                    dve.wait_ge(sem("attT_mm"), q)
                v.tensor_tensor(by(o_nat, HEADS), by(bank(6), HEADS),
                                ast[:, 5, :].unsqueeze(2).broadcast_to([P, HEADS, HD]), ALU.mult) \
                    .then_inc(sem("o_ready"), 1)
            dve.wait_ge(sem("attT_mm"), TT)

            dve.sem_inc(sem("kk_raw"), 1)
            for m in range(PAIRS):
                s(v.tensor_scalar(head_rk[:, m * P:(m + 1) * P], head_ones, pcol[:, RKC + m:RKC + m + 1], None,
                                  ALU.mult))
            dve.sem_inc(sem("bonus_in"), 1)
            dve.wait_ge(sem("kk_norm"), 4)
            nrm = at(X0, 8 * KB)
            s(v.tensor_scalar(nrm, nrm, 1e-12, None, ALU.max))
            s(v.reciprocal(nrm, nrm))
            s(v.tensor_tensor(KKt, KKt, nrm, ALU.mult))
            dve.wait_ge(sem("exp_lc"), 1)
            pcv = Pc.rearrange("p (s d m) -> p d m s", s=STEPS, d=DIRS)
            e5 = E_.rearrange("p (d m s t) -> p d m s t", d=DIRS, m=PAIRS, s=STEPS)
            s(v.tensor_copy(pcv[:, 0], e5[:, 0, :, :, CHUNK - 1]))
            for st in range(STEPS):
                s(v.tensor_copy(pcv[:, 1, :, st], e5[:, 1, :, STEPS - 1 - st, 0]))
            dve.sem_inc(sem("Pc_ready"), 1)
            for d in range(DIRS):
                h = slice(d * 2048, (d + 1) * 2048)
                s(v.tensor_tensor(A_[:, h], A_[:, h], KKt, ALU.mult))
            dve.wait_ge(sem("exp_lcw"), 1)
            for d in range(DIRS):
                h = slice(d * 2048, (d + 1) * 2048)
                s(v.scalar_tensor_tensor(LW[:, h], LW[:, h], -1.0, KKt, ALU.mult, ALU.mult))
            dve.wait_ge(sem("exp_neg"), 1)
            s(v.tensor_tensor(A_, A_, LC, ALU.mult))
            for m in range(PAIRS):
                dve.wait_ge(sem("bonus_mm"), m + 1)
                s(v.tensor_tensor(by(BON, 4)[:, m, :], bank(4 + m), by(Vt, 4)[:, m, :], ALU.mult))
            dve.sem_inc(sem("prep_done"), 1)

            B = {n: bd(t) for n, t in tile.items()}
            S_bd = bd(state)
            dve.wait_ge(sem("mod_rows_out"), 16)
            s(v.memset(state, 0.0))
            dve.sem_inc(sem("state_ready"), 2)
            Q = tile["Qs"].rearrange("p (d w m t) -> p w d m t", w=2, d=DIRS, m=PAIRS)
            with dve.Fori(0, STEPS) as i:
                def masked(name, dst, mask):
                    for d in range(DIRS):
                        scan_product(dve, i, name, d)
                        v.tensor_tensor(B[dst][:, d], by(scan_bank(name, d), PAIRS),
                                        mask[:, d * P:(d + 1) * P].unsqueeze(1).broadcast_to([P, PAIRS, P]),
                                        ALU.mult).then_inc(sem("scan_vecs"), 1)

                def masked_halves(name, dst, mask):
                    for d in range(DIRS):
                        scan_product(dve, i, name, d)
                        v.tensor_tensor(B[dst][:, d].rearrange("p m (h t) -> p m h t", h=2),
                                        by(scan_bank(name, d), PAIRS)[:, :, 0:CHUNK].unsqueeze(2)
                                        .broadcast_to([P, PAIRS, 2, CHUNK]),
                                        by(mask[:, d * P:(d + 1) * P], 2).unsqueeze(1)
                                        .broadcast_to([P, PAIRS, 2, CHUNK]),
                                        ALU.mult).then_inc(sem("scan_vecs"), 1)

                def masked_rho(name, w):
                    for d in range(DIRS):
                        scan_product(dve, i, name, d)
                        v.tensor_tensor(Q[:, w, d], by(scan_bank(name, d), PAIRS)[:, :, CHUNK:2 * CHUNK],
                                        mask_QT[:, d * 64:(d + 1) * 64].unsqueeze(1)
                                        .broadcast_to([P, PAIRS, CHUNK]),
                                        ALU.mult).then_inc(sem("scan_vecs"), 1)

                def plus(name, dst, add):
                    for d in range(DIRS):
                        scan_product(dve, i, name, d)
                        v.tensor_tensor(B[dst][:, d], by(scan_bank(name, d), PAIRS), B[add][:, d], ALU.add) \
                            .then_inc(sem("scan_vecs"), 1)

                masked("A", "D1", mask_D)
                masked_halves("B", "D1T", mask_DT)
                masked("A", "Fm", mask_F)
                for d in range(DIRS):
                    scan_made(dve, i, "DT", d)
                    v.tensor_tensor(B["Pt"][:, d], B["D1T"][:, d],
                                    ident.unsqueeze(1).broadcast_to([P, PAIRS, P]), ALU.add) \
                        .then_inc(sem("scan_vecs"), 1)
                masked_rho("B", 0)
                masked_halves("C", "AkT", mask_AT)
                masked_rho("C", 1)
                plus("P2", "Pt", "Pt")
                plus("P4", "Pt", "Pt")
                plus("P8", "Pt", "Pt")
                for d in range(DIRS):
                    scan_made(dve, i, "U1", d)
                plus("Ua", "D1", "D1T")
                plus("Ub", "D2", "D1T")
                plus("U", "Fm", "D1T")
                for d in range(DIRS):
                    scan_product(dve, i, "SU", d)
                    v.tensor_tensor(S_bd[:, d], by(scan_bank("SU", d), PAIRS), S_bd[:, d], ALU.add) \
                        .then_inc(sem("scan_vecs"), 1)
                for d in range(DIRS):
                    scan_made(dve, i, "Ssum", d)
                    pc = Pc[:, bass.ds(i * DIRS * PAIRS + d * PAIRS, PAIRS)]
                    v.tensor_tensor(S_bd[:, d], S_bd[:, d], pc.unsqueeze(2).broadcast_to([P, PAIRS, P]),
                                    ALU.mult).then_inc(sem("state_ready"), 1)

            dve.wait_ge(sem("y_free"), 2 * STEPS + 2)
            dve.wait_ge(sem("scan_mm"), 2 * len(p_names) * (STEPS + 1))
            dve.sem_inc(sem("scan_done"), 1)
            y = yT[:, 0:8 * KB]
            s(v.tensor_tensor(y, y, yT[:, 8 * KB:16 * KB], ALU.add))
            dve.sem_inc(sem("y_sum"), 1)
            for m in range(PAIRS):
                dve.wait_ge(sem("gn_mean_mm"), m + 1)
                s(v.scalar_tensor_tensor(by(y, 4)[:, m, :], bank(m), -1.0 / RN, by(y, 4)[:, m, :], ALU.mult, ALU.add))
            dve.sem_inc(sem("gn_centred"), 1)
            for m in range(PAIRS):
                dve.wait_ge(sem("gn_var_mm"), m + 1)
                v.tensor_scalar(by(gn_tmp, 4)[:, m, :], bank(4 + m), 1.0 / RN, GN_EPS, ALU.mult, ALU.add) \
                    .then_inc(sem("gn_vare"), 1)
            dve.wait_ge(sem("gn_std"), 1)
            s(v.reciprocal(gn_tmp, gn_tmp))
            s(v.tensor_tensor(rwT, y, gn_tmp, ALU.mult))
            dve.sem_inc(sem("gn_done"), 1)
            for m in range(PAIRS):
                s(v.tensor_scalar(by(rwT, 4)[:, m, :], by(rwT, 4)[:, m, :], pcol[:, LG + m:LG + m + 1],
                                  pcol[:, LB + m:LB + m + 1], ALU.mult, ALU.add))
            s(v.tensor_tensor(rwT, rwT, BON, ALU.add))
            v.tensor_tensor(rwT, rwT, GG, ALU.mult).then_inc(sem("rwT_ready"), 1)
            tmp = [at(40, T), at(42, T)]
            gv = by(gates, GATEB)
            dve.wait_ge(sem("gate_ready"), 4)
            for m in range(KC):
                dve.wait_ge(sem("mix_mm"), m + 1)
                if m:
                    dve.wait_ge(sem("mixT_ready"), m)
                s(v.tensor_tensor(tmp[0], gv[:, m, :], bank(m % 4), ALU.mult))
                s(v.tensor_tensor(tmp[1], gv[:, KC + m, :], bank(4 + m % 4), ALU.mult))
                v.tensor_tensor(by(mixT, KC)[:, m, :], tmp[0], tmp[1], ALU.add).then_inc(sem("mixT_ready"), 1)
            dve.wait_ge(sem("rows_in"), 80)
            t1 = at(128, D)
            dve.wait_ge(sem("n2_in"), 16)
            s(v.scalar_tensor_tensor(s2b, s2b, 1.0, n2b, ALU.add, ALU.mult))
            for t in range(TT):
                dve.wait_ge(sem("out_mm"), t + 1)
                if t:
                    dve.wait_ge(sem("x2_ready"), t)
                s(v.tensor_tensor(t1, psum[:, 1024 * t:1024 * t + 1024], gt1b, ALU.mult))
                v.tensor_tensor(by(x2, TT)[:, t, :], by(x2, TT)[:, t, :], t1, ALU.add) \
                    .then_inc(sem("x2_ready"), 1)
                dve.wait_ge(sem("x2_sq"), t + 1)
                v.tensor_scalar(stat[:, 12 + t:13 + t], stat[:, 8 + t:9 + t], 1.0 / D, RMS_EPS,
                                ALU.mult, ALU.add).then_inc(sem("x2_ms"), 1)
                dve.wait_ge(sem("x2_rms"), t + 1)
                s(v.reciprocal(stat[:, 20 + t:21 + t], stat[:, 16 + t:17 + t]))
                s(v.scalar_tensor_tensor(by(h2, TT)[:, t, :], by(x2, TT)[:, t, :], stat[:, 20 + t:21 + t], s2b,
                                         ALU.mult, ALU.mult))
                v.tensor_tensor(by(h2, TT)[:, t, :], by(h2, TT)[:, t, :], sh2b, ALU.add) \
                    .then_inc(sem("h2_ready"), 1)
            dve.wait_ge(sem("router_mm"), TT)
            lg = psum.rearrange("p (t n) -> p t n", t=TT)[:, :, 0:NE]
            mx = stat[:, 40:44]
            s(v.tensor_reduce(mx, lg, AX.X, ALU.max))
            v.tensor_tensor(by(affs, TT), lg, mx.unsqueeze(2).broadcast_to([P, TT, NE]), ALU.subtract) \
                .then_inc(sem("lg_ready"), 1)
            dve.sem_inc(sem("route_lg_done"), 1)
            dve.wait_ge(sem("aff_exp"), 1)
            s(v.tensor_reduce(stat[:, 44:48], by(affs, TT), AX.X, ALU.add))
            s(v.reciprocal(stat[:, 44:48], stat[:, 44:48]))
            v.tensor_tensor(by(aff, TT), by(affs, TT), stat[:, 44:48].unsqueeze(2).broadcast_to([P, TT, NE]),
                            ALU.mult).then_inc(sem("aff_ready"), 1)
            dve.wait_ge(sem("affT_ready"), 1)
            for r in range(SLOTS // 8):
                src = affT if r == 0 else work
                s(v.max(top8, src))
                s(v.match_replace(work, top8, src, -1.0))
            s(v.tensor_scalar(chosen, work, 0.0, None, ALU.is_lt))
            s(v.memset(work, 1.0))
            s(v.tensor_tensor_scan(count, work, chosen, 0.0, ALU.mult, ALU.add))
            s(v.tensor_tensor(count, count, chosen, ALU.mult))
            v.tensor_scalar(count, count, -1.0, None, ALU.add).then_inc(sem("rank_ready"), 1)
            dve.wait_ge(sem("rankT_mm"), 1)
            s(v.tensor_copy(rankT, bank(1)[:, 0:TT * NE]))
            s(v.memset(macc, 0.0))
            dve.sem_inc(sem("macc_ready"), 8)
            with dve.Fori(0, EPAIRS) as i:
                for e in range(2):
                    for t in range(TT):
                        ins = v.tensor_scalar(by(pick, TT)[:, t, e * SLOTS:(e + 1) * SLOTS], slot_row,
                                              rankT[:, bass.ds(2 * i + t * NE + e, 1)], None, ALU.is_equal)
                ins.then_inc(sem("pick_ready"), 1)
                dve.wait_ge(sem("pair_rows_in"), 64 * i + 64)
                v.scalar_tensor_tensor(put, rank_b, slot_col[:, 0:1], gate_b, ALU.is_equal, ALU.mult) \
                    .then_inc(sem("put_ready"), 1)
                for n in range(4):
                    c = slice(n * 512, (n + 1) * 512)
                    dve.wait_ge(sem("sig_ready"), 4 * i + n + 1)
                    v.tensor_tensor(hid[:, c], sig[:, c], bank(n), ALU.mult).then_inc(sem("silu_ready"), 1)
                dve.wait_ge(sem("ring_used"), PER_PAIR * i + 32)
                for n in range(4):
                    c = slice(n * 512, (n + 1) * 512)
                    dve.wait_ge(sem("silu_ready"), 4 * i + n + 1)
                    v.tensor_tensor(hid[:, c], hid[:, c], bank(4 + n), ALU.mult).then_inc(sem("hid_ready"), 1)
                for t in range(TT):
                    for n in range(2):
                        c = t * D + n * 512
                        dve.wait_ge(sem("put_mm"), 8 * i + 2 * t + n + 1)
                        v.tensor_tensor(macc[:, c:c + 512], macc[:, c:c + 512], bank((6 + 2 * t + n) % 8), ALU.add) \
                            .then_inc(sem("macc_ready"), 1)
            dve.wait_ge(sem("macc_ready"), 8 * EPAIRS + 8)
            dve.wait_ge(sem("gt2_in"), 16)
            for t in range(TT):
                s(v.tensor_tensor(by(macc, TT)[:, t, :], by(macc, TT)[:, t, :], gt2_keep, ALU.mult))
                v.tensor_tensor(by(x2, TT)[:, t, :], by(x2, TT)[:, t, :], by(macc, TT)[:, t, :], ALU.add) \
                    .then_inc(sem("x3_ready"), 1)
            dve.wait_ge(sem("x3_sq"), TT)
            s(rstd(None, "x3_ms", "x3_rms", 24))
            dve.wait_ge(sem("fin_in"), 16)
            dve.wait_ge(sem("xe_ready"), 2 * EPAIRS)
            for t in range(TT):
                v.scalar_tensor_tensor(by(h2, TT)[:, t, :], by(x2, TT)[:, t, :], stat[:, 36 + t:37 + t], fin_b,
                                       ALU.mult, ALU.mult).then_inc(sem("final_ready"), 1)


_INS = ["x", "c", "norm1_g", "norm2_g", "ada_w", "ada_b", "w_in", "attn_sink", "shift_mu", "decay_w0",
        "decay_w2", "iclr_a0", "iclr_a2", "gate_g2", "k_k", "k_a", "r_k", "lnx_g", "lnx_b", "w_br_attn",
        "w_br_rwkv", "w_out", "router_w", "exp_w_gate", "exp_w_up", "exp_w_down", "final_g"]


def kernel(**inputs):
    import numpy as _np
    import concourse.bacc as _bacc
    from concourse import mybir as _mybir
    from concourse.bass_utils import run_bass_kernel_spmd as _run

    nc = _bacc.Bacc("TRN2", target_bir_lowering=False, num_devices=1)
    arrays, args = {}, []
    for name in _INS:
        a = _np.ascontiguousarray(inputs[name])
        arrays[f"in_{name}_dram"] = a
        args.append(nc.dram_tensor(f"in_{name}_dram", a.shape, _mybir.dt.from_np(a.dtype), kind="ExternalInput").ap())
    args.append(nc.dram_tensor("out_dram", (1, T, D), F32, kind="ExternalOutput").ap())
    hybrid_layer(nc, *args)
    r = _run(nc, [arrays], core_ids=[0])
    return r.results[0]["out_dram"]
```
